# Optimizing a Trainium2 kernel written in Bass

```python
import jax, jax.numpy as jnp
from jax import lax
import numpy as np

D_MODEL = 1024
BATCH = 1
SEQ = 256
DEPTH = 2

GMLP_CHUNK = 128
GMLP_GROUPS = 8
GMLP_GROUP_DIM = 128
GMLP_WIDTH = GMLP_GROUPS * GMLP_GROUP_DIM
HGRN_HEADS = 8
HGRN_DK = 128
HGRN_DV = 128
HGRN_KWIDTH = HGRN_HEADS * HGRN_DK
HGRN_VWIDTH = HGRN_HEADS * HGRN_DV
HGRN_CHUNK = 64
FFN_HIDDEN = 2816
N_ADA = 9
EPS = 1e-6
IN_SPLITS = (GMLP_WIDTH, GMLP_WIDTH,
             HGRN_KWIDTH, HGRN_KWIDTH,
             HGRN_VWIDTH, HGRN_VWIDTH,
             D_MODEL, D_MODEL)
IN_WIDTH = sum(IN_SPLITS)

kernel_name = 'hybrid_gmlp_hgrn2_macaron_adaln'

def _rms_norm(x, w):
    xf = x.astype(jnp.float32)
    y = xf * lax.rsqrt(jnp.mean(xf * xf, axis=-1, keepdims=True) + EPS)
    return (y * w.astype(jnp.float32)).astype(x.dtype)

def _split_cols(z, widths):
    idx = [int(v) for v in np.cumsum(widths)[:-1]]
    return jnp.split(z, idx, axis=-1)

def _swiglu(xn, w13, w2):
    a, b = jnp.split(xn @ w13, 2, axis=-1)
    return (jax.nn.silu(a) * b) @ w2

def _gmlp_branch(u, v, ws, bs):
    b, s, _ = v.shape
    nc = s // GMLP_CHUNK
    vg = v.reshape(b, nc, GMLP_CHUNK, GMLP_GROUPS, GMLP_GROUP_DIM).astype(jnp.float32)
    mu = jnp.mean(vg, axis=-1, keepdims=True)
    var = jnp.mean(jnp.square(vg - mu), axis=-1, keepdims=True)
    vn = ((vg - mu) * lax.rsqrt(var + EPS)).astype(v.dtype)
    ws_causal = jnp.tril(ws)
    mixed = jnp.einsum('gts,bnsgc->bntgc', ws_causal, vn) + bs.T[None, None, :, :, None]
    return u * mixed.reshape(b, s, GMLP_WIDTH)

def _to_chunks(t, heads, d):
    b, s, _ = t.shape
    return t.reshape(b, s // HGRN_CHUNK, HGRN_CHUNK, heads, d).transpose(1, 0, 3, 2, 4)

def _hgrn2_branch(q_pre, f_pre, i_in, og, lb):
    b, s, _ = q_pre.shape
    lb = lb.astype(jnp.float32)
    fz = f_pre.astype(jnp.float32)
    q = jax.nn.silu(q_pre.astype(jnp.float32))
    logf = jnp.logaddexp(jnp.log(lb), jnp.log1p(-lb) + jax.nn.log_sigmoid(fz))
    k = (1.0 - lb) * jax.nn.sigmoid(-fz)
    v = i_in.astype(jnp.float32)

    qc = _to_chunks(q, HGRN_HEADS, HGRN_DK)
    kc = _to_chunks(k, HGRN_HEADS, HGRN_DK)
    vc = _to_chunks(v, HGRN_HEADS, HGRN_DV)
    bcum = jnp.cumsum(_to_chunks(logf, HGRN_HEADS, HGRN_DK), axis=3)
    causal = jnp.tril(jnp.ones((HGRN_CHUNK, HGRN_CHUNK), dtype=bool))

    def step(state, inp):
        q_t, k_t, v_t, b_t = inp
        diff = b_t[:, :, :, None, :] - b_t[:, :, None, :, :]
        decay = jnp.exp(jnp.where(causal[:, :, None], diff, -jnp.inf))
        scores = jnp.einsum('bhtk,bhsk,bhtsk->bhts', q_t, k_t, decay)
        o = jnp.einsum('bhts,bhsv->bhtv', scores, v_t) + \
            jnp.einsum('bhtk,bhkv->bhtv', q_t * jnp.exp(b_t), state)
        b_last = b_t[:, :, -1:, :]
        new_state = jnp.exp(b_last[:, :, 0, :])[..., None] * state + \
            jnp.einsum('bhsk,bhsv->bhkv', k_t * jnp.exp(b_last - b_t), v_t)
        return new_state, o

    s0 = jnp.zeros((b, HGRN_HEADS, HGRN_DK, HGRN_DV), jnp.float32)
    _, o = lax.scan(step, s0, (qc, kc, vc, bcum))
    o = o.transpose(1, 0, 3, 2, 4).reshape(b, s, HGRN_HEADS, HGRN_DV)
    o = o * lax.rsqrt(jnp.mean(o * o, axis=-1, keepdims=True) + EPS)
    o = o.reshape(b, s, HGRN_VWIDTH) * jax.nn.sigmoid(og.astype(jnp.float32))
    return o.astype(q_pre.dtype)

def _mixer(hn, w_in, ws, bs, lb, w_a, w_b, w_o):
    z = hn @ w_in
    u, v, q, fz, i_in, og, ga, gb = _split_cols(z, IN_SPLITS)
    ya = _gmlp_branch(jax.nn.gelu(u), jax.nn.gelu(v), ws, bs) @ w_a
    yb = _hgrn2_branch(q, fz, i_in, og, lb) @ w_b
    m = jax.nn.sigmoid(ga) * ya + jax.nn.sigmoid(gb) * yb
    return m @ w_o

def setup_inputs(seed: int = 0) -> dict:
    key = jax.random.key(seed)
    ks = jax.random.split(key, 15)
    nrm = jax.random.normal
    f32 = jnp.float32
    return {
        'x': nrm(ks[0], (BATCH, SEQ, D_MODEL), f32),
        'c': nrm(ks[1], (BATCH, D_MODEL), f32),
        'w_in': nrm(ks[2], (DEPTH, D_MODEL, IN_WIDTH), f32) * D_MODEL ** -0.5,
        'gmlp_ws': nrm(ks[3], (DEPTH, GMLP_GROUPS, GMLP_CHUNK, GMLP_CHUNK), f32) * (0.5 * GMLP_CHUNK ** -0.5),
        'gmlp_b': 1.0 + 0.1 * nrm(ks[4], (DEPTH, GMLP_GROUPS, GMLP_CHUNK), f32),
        'hgrn_lb_logits': 0.5 * nrm(ks[5], (DEPTH, HGRN_KWIDTH), f32),
        'w_branch_a': nrm(ks[6], (DEPTH, GMLP_WIDTH, D_MODEL), f32) * GMLP_WIDTH ** -0.5,
        'w_branch_b': nrm(ks[7], (DEPTH, HGRN_VWIDTH, D_MODEL), f32) * HGRN_VWIDTH ** -0.5,
        'w_out': nrm(ks[8], (DEPTH, D_MODEL, D_MODEL), f32) * D_MODEL ** -0.5,
        'ffn_w13': nrm(ks[9], (DEPTH, 2, D_MODEL, 2 * FFN_HIDDEN), f32) * D_MODEL ** -0.5,
        'ffn_w2': nrm(ks[10], (DEPTH, 2, FFN_HIDDEN, D_MODEL), f32) * FFN_HIDDEN ** -0.5,
        'norm_w': 1.0 + 0.05 * nrm(ks[11], (DEPTH, 3, D_MODEL), f32),
        'ada_w': nrm(ks[12], (DEPTH, D_MODEL, N_ADA * D_MODEL), f32) * (0.1 * D_MODEL ** -0.5),
        'ada_b': 0.02 * nrm(ks[13], (DEPTH, N_ADA * D_MODEL), f32),
        'final_norm_w': 1.0 + 0.05 * nrm(ks[14], (D_MODEL,), f32),
    }

def reference(x, c, w_in, gmlp_ws, gmlp_b, hgrn_lb_logits, w_branch_a, w_branch_b, w_out,
              ffn_w13, ffn_w2, norm_w, ada_w, ada_b, final_norm_w):
    lb_all = jnp.cumsum(jax.nn.softmax(hgrn_lb_logits.astype(jnp.float32), axis=0), axis=0)
    lb_all = lb_all - lb_all[0:1]
    c_act = jax.nn.silu(c)
    h = x
    for l in range(DEPTH):
        mod = (c_act @ ada_w[l] + ada_b[l]).reshape(c.shape[0], N_ADA, 1, D_MODEL)
        sh1, sc1, g1, sh2, sc2, g2, sh3, sc3, g3 = [mod[:, j] for j in range(N_ADA)]
        hn = _rms_norm(h, norm_w[l, 0]) * (1.0 + sc1) + sh1
        h = h + 0.5 * (1.0 + g1) * _swiglu(hn, ffn_w13[l, 0], ffn_w2[l, 0])
        hn = _rms_norm(h, norm_w[l, 1]) * (1.0 + sc2) + sh2
        h = h + (1.0 + g2) * _mixer(hn, w_in[l], gmlp_ws[l], gmlp_b[l], lb_all[l],
                                    w_branch_a[l], w_branch_b[l], w_out[l])
        hn = _rms_norm(h, norm_w[l, 2]) * (1.0 + sc3) + sh3
        h = h + 0.5 * (1.0 + g3) * _swiglu(hn, ffn_w13[l, 1], ffn_w2[l, 1])
    return _rms_norm(h, final_norm_w)


_drawn_inputs = setup_inputs


def setup_inputs(seed=0):
    import zlib

    import numpy as np

    out = dict(_drawn_inputs(seed))
    spreads = {}
    factors = {'hgrn_lb_logits': 4.378}
    for name, (base, spread) in spreads.items():
        noise = np.random.default_rng([zlib.crc32(name.encode()), seed]).standard_normal(out[name].shape)
        drawn = base * np.exp(spread * noise) if base else spread * noise
        out[name] = __import__('jax').numpy.asarray(drawn.astype(out[name].dtype))
    for name, factor in factors.items():
        out[name] = (out[name] * factor).astype(out[name].dtype)
    return out
```

```python
from contextlib import ExitStack

import numpy as np

import concourse.bass as bass
from concourse import mybir

F32 = mybir.dt.float32
F32R = mybir.dt.float32r
U8 = mybir.dt.uint8
ALU = mybir.AluOpType
ACT = mybir.ActivationFunctionType

P = 128
DEPTH = 2
D = 1024
T = 256
KT = D // P
NT = T // P
HID = 2816
HT = HID // P
EPS = 1e-6
HEADS = 8
N_ADA = 9

RING = 4
CHUNK = 1024
KC = 4
JC = 256
PAIRS = HID // JC
ADA_BLOCKS = N_ADA * D // 256

FFN_CHUNKS = 4 * PAIRS + HT
SEGMENTS = (3, 2, 1, 0, 4, 5, 6, 7)
GROUPS = 16
MIX_CHUNKS = 4 * GROUPS + 3 * 8
LAYER_CHUNKS = 2 * FFN_CHUNKS + MIX_CHUNKS
ALL_CHUNKS = DEPTH * LAYER_CHUNKS
FFN_JOBS = 2 * PAIRS
PROJ_JOBS = 2 * GROUPS
MIX_JOBS = PROJ_JOBS + 12
LAYER_JOBS = 2 * FFN_JOBS + MIX_JOBS

LEVELS = (1, 2, 4, 8, 16, 32, 64)
MIX_READS = 2 + 4 * (1 + len(LEVELS)) + 4 + 2
ADA_PLAN = {0: (8, 11, 2, 3), 1: (36, 11, 2, 1), 2: (58, 11, 0, 3), 3: (72, 0, 0, 0)}
ADA_MIX = (32, 4)

ROW_C, ROW_LB, ROW_NW, ROW_FN, ROWS = 0, 8, 24, 72, 80


def trunk(nc, x, c, w_in, gmlp_ws, gmlp_b, lb_logits, w_a, w_b, w_o, w13, w2, norm_w, ada_w, ada_b,
          final_w, ident_in, level_mask_in, tril_in, out):
    ctx = ExitStack()
    with ctx:
        def sb(name, shape, dt=F32, stack=ctx):
            return stack.enter_context(nc.sbuf_tensor(name, shape, dt))

        def sem(name):
            return ctx.enter_context(nc.semaphore(name))

        raw = sb("raw", [P, RING, CHUNK])
        w_hi = sb("w_hi", [P, RING, CHUNK], F32R)
        w_lo = sb("w_lo", [P, RING, CHUNK], F32R)
        ada_raw = sb("ada_raw", [P, 2, KT, 256])
        ada_acc = sb("ada_acc", [P, 2, 256])
        ada_mix = sb("ada_mix", [P, 4, 256])
        h = sb("h", [P, KT, T])
        x_hi = sb("x_hi", [P, KT, T], F32R)
        x_lo = sb("x_lo", [P, KT, T], F32R)
        mod = sb("mod", [P, DEPTH * N_ADA * KT])
        params = sb("params", [P, ROWS])
        adab = sb("adab", [P, DEPTH * N_ADA * KT])
        c_act = sb("c_act", [P, KT])
        scale_a = sb("scale_a", [P, KT])
        coef = sb("coef", [P, KT])
        rstd = sb("rstd", [P, T])
        ones = sb("ones", [P, P])
        eps_t = sb("eps_t", [P, 2])
        ident = sb("ident", [P, P])
        tril = sb("tril", [P, P])
        level_mask = sb("level_mask", [P, len(LEVELS), P], U8)
        lb_t = sb("lb_t", [P, 6, HEADS])
        bias_row = sb("bias_row", [1, HEADS, P])
        ln_stats = sb("ln_stats", [P, 16, 6])
        ln_mv = sb("ln_mv", [P, 16, 2])
        ln_rstd = sb("ln_rstd", [P, 16])
        ws_t = sb("ws_t", [P, HEADS, P])

        with ExitStack() as tmp:
            silu_a = sb("silu_a", [P, 2, 512], F32, tmp)
            gated = sb("gated", [P, 2, 512], F32, tmp)
        norm_tmp = sb("norm_tmp", [P, KT, T])

        with ExitStack() as tmp:
            g_hi = sb("g_hi", [P, HT, T], F32R, tmp)
            g_lo = sb("g_lo", [P, HT, T], F32R, tmp)
        def unit(name, dt=F32, stack=ctx):
            return sb(name, [P, KT, T], dt, stack)
        with ExitStack() as tmp:
            rows_in = sb("rows_in", [P, 3, P], F32, tmp)
            x_in = sb("x_in", [P, NT, D], F32, tmp)
            mask_in = sb("mask_in", [P, len(LEVELS), P], F32, tmp)
            y_out = sb("y_out", [P, NT, D], F32, tmp)
            y_t = sb("y_t", [P, KT, T], F32, tmp)
        with ExitStack() as tmp:
            yb_hi = unit("yb_hi", F32R, tmp)
            yb_lo = unit("yb_lo", F32R, tmp)
        key = unit("key")
        query = unit("query")
        logf = unit("logf")
        pair = unit("pair")
        decay = unit("decay")
        score = unit("score")
        val = unit("val")
        with ExitStack() as tmp:
            v_gate = unit("v_gate", F32, tmp)
        ya_hi = unit("ya_hi", F32R)
        u_gate = unit("u_gate")
        ya_lo = unit("ya_lo", F32R)
        ga = unit("ga")
        ws_raw = sb("ws_raw", [P, HEADS, P])
        o_t, gb, og = logf, pair, u_gate
        sq_o, rms_o = key, query

        bank = [ctx.enter_context(nc.psum_tensor(f"bank{i}", [P, 512], F32)) for i in range(8)]

        raw_landed = [sem(f"raw_landed{i}") for i in range(RING)]
        hi_ready, lo_ready, chunk_used = (sem(n) for n in ("hi_ready", "lo_ready", "chunk_used"))
        gate_free, up_free = sem("gate_free"), sem("up_free")
        g_hi_ready, g_lo_ready = sem("g_hi_ready"), sem("g_lo_ready")
        proj_taken, branch_taken = sem("proj_taken"), sem("branch_taken")
        small_landed, x_landed, const_landed = sem("small_landed"), sem("x_landed"), sem("const_landed")
        ws_landed, bias_landed = sem("ws_landed"), sem("bias_landed")
        ones_ready, consts_ready, setup_v = sem("ones_ready"), sem("consts_ready"), sem("setup_v")
        rows_turned, params_ready, c_ready = sem("rows_turned"), sem("params_ready"), sem("c_ready")
        x_turned, h_loaded = sem("x_turned"), sem("h_loaded")
        ada_landed = [sem("ada_landed0"), sem("ada_landed1")]
        ada_summed, ada_reduced, mod_ready = sem("ada_summed"), sem("ada_reduced"), sem("mod_ready")
        h_ready, sq_ready, sum_ready, rms_ready = sem("h_ready"), sem("sq_ready"), sem("sum_ready"), sem("rms_ready")
        t_ready, x_hi_ready, x_lo_ready, vv = sem("t_ready"), sem("x_hi_ready"), sem("x_lo_ready"), sem("vv")
        aa = sem("aa")
        softmax_v, softmax_a = sem("softmax_v"), sem("softmax_a")
        ws_masked, mix_scored, mix_read = sem("ws_masked"), sem("mix_scored"), sem("mix_read")
        f_act, f_vec = sem("f_act"), sem("f_vec")
        suffix_ready, decay_ready, pair_ready = sem("suffix_ready"), sem("decay_ready"), sem("pair_ready")
        ln_var, ln_std, v_norm = sem("ln_var"), sem("ln_std"), sem("v_norm")
        ya_hi_ready, ya_lo_ready = sem("ya_hi_ready"), sem("ya_lo_ready")
        o_done, o_taken, o_summed, o_rms = sem("o_done"), sem("o_taken"), sem("o_summed"), sem("o_rms")
        yb_full, yb_hi_ready, yb_lo_ready = sem("yb_full"), sem("yb_hi_ready"), sem("yb_lo_ready")
        m_full, m_hi_ready, m_lo_ready = sem("m_full"), sem("m_hi_ready"), sem("m_lo_ready")
        y_ready, y_turned, y_copied, y_stored = sem("y_ready"), sem("y_turned"), sem("y_copied"), sem("y_stored")

        def ffn_chunk0(f):
            return (f // 2) * LAYER_CHUNKS + (f % 2) * (FFN_CHUNKS + MIX_CHUNKS)

        def ffn_job0(f):
            return (f // 2) * LAYER_JOBS + (f % 2) * (FFN_JOBS + MIX_JOBS)

        def mix_chunk0(l):
            return l * LAYER_CHUNKS + FFN_CHUNKS

        def mix_job0(l):
            return l * LAYER_JOBS + FFN_JOBS

        def job_bank(j):
            return bank[4 + j % 4]

        norm_bank = {0: bank[2], 1: bank[7], 2: bank[0], 3: bank[7], 4: bank[7], 5: bank[0], 6: bank[7]}

        def halves(t, m):
            flat = t[:, :, :].rearrange("p h t -> p (h t)")
            return flat.rearrange("p (b two m) -> p b two m", two=2, m=m)

        block = ctx.enter_context(nc.Block())

        w13_v = w13.rearrange("l w (q k p) c -> l w q p k c", k=KC, p=P)
        w2_v = w2.rearrange("l w (k p) c -> l w p k c", p=P)
        in_v = w_in.rearrange("l (q k p) c -> l q p k c", k=KC, p=P)
        mix_v = [w.rearrange("l (q k p) c -> l q p k c", k=KC, p=P) for w in (w_a, w_b, w_o)]

        @block.sync
        def _(sp):
            def load(slot, src, wait):
                if wait is not None:
                    sp.wait_ge(lo_ready, wait)
                dst = raw[:, slot, :]
                if len(src.shape) == 3:
                    dst = dst.rearrange("p (k c) -> p k c", k=KC)
                sp.dma_start(dst, src).then_inc(raw_landed[slot], 16)

            def ffn(f):
                l, w, c0 = f // 2, f % 2, ffn_chunk0(f)

                def pair_loads(p, first):
                    for i in range(4):
                        col = p * JC + (i // 2) * HID
                        load((c0 + i) % RING, w13_v[l, w, i % 2][:, :, bass.ds(col, JC)],
                             None if first else c0 + 4 * p + i - RING + 1)
                if f == 0:
                    pair_loads(0, True)
                    with sp.Fori(1, PAIRS) as p:
                        pair_loads(p, False)
                else:
                    with sp.Fori(0, PAIRS) as p:
                        pair_loads(p, False)
                d0 = c0 + 4 * PAIRS
                with sp.Fori(0, HT // 4) as t:
                    for i in range(4):
                        load((d0 + i) % RING, w2_v[l, w][:, bass.ds(4 * t + i, 1), :].rearrange("p k c -> p (k c)"),
                             d0 + 4 * t + i - RING + 1)
                for k in range(HT // 4 * 4, HT):
                    load((d0 + k) % RING, w2_v[l, w][:, k, :], d0 + k - RING + 1)

            def mixer(l):
                c0 = mix_chunk0(l)
                for half in range(2):
                    with sp.Fori(0, 4) as s:
                        first = s * D + 4 * D if half else s * -D + 3 * D
                        for i in range(8):
                            at = c0 + 32 * half + i
                            load(at % RING, in_v[l, i % 2][:, :, bass.ds(first + (i // 2) * JC, JC)],
                                 at + 8 * s - RING + 1)
                for b in range(3):
                    for i in range(8):
                        at = c0 + 64 + 8 * b + i
                        load(at % RING, mix_v[b][l, i % 2][:, :, (i // 2) * JC:(i // 2 + 1) * JC], at - RING + 1)

            for l in range(DEPTH):
                ffn(2 * l)
                mixer(l)
                ffn(2 * l + 1)
            for n in range(NT):
                sp.wait_ge(y_copied, 4 * (n + 1))
                sp.dma_start(out[0, n * P:(n + 1) * P, :], y_out[:, n, :]).then_inc(y_stored, 16)
            sp.wait_ge(y_stored, 16 * NT)

        ada_v = ada_w.rearrange("l (k p) c -> l p k c", p=P)

        @block.gpsimd
        def _(pool):
            def ada_load(n, blk, parity, wait=True):
                if wait:
                    pool.wait_ge(ada_summed, KT * n - KT)
                l, b = blk
                pool.dma_start(ada_raw[:, parity, :, :], ada_v[l][:, :, bass.ds(b * 256, 256)]).then_inc(ada_landed[parity], 16)

            def ws_load(l):
                if l:
                    pool.wait_ge(mix_read, MIX_READS * l)
                    pool.wait_ge(mix_scored, MIX_READS * l)
                pool.dma_start(ws_raw[:, :, :], gmlp_ws[l].rearrange("g t s -> t g s")).then_inc(ws_landed, 16)
                pool.dma_start(bias_row[:, :, :], gmlp_b[l:l + 1]).then_inc(bias_landed, 16)

            for n in range(8):
                ada_load(n, (0, n), n % 2, n >= 2)
            ws_load(0)

            def ada_phase(f):
                n0, in_w13, per_loop, rest = ADA_PLAN[f]
                l, b0 = n0 // ADA_BLOCKS, n0 % ADA_BLOCKS
                if not in_w13:
                    return
                count = in_w13 + 5 * per_loop + rest
                with pool.Fori(0, count // 2) as t:
                    for i in range(2):
                        ada_load(n0 + 2 * t + i, (l, b0 + 2 * t + i), i)
                if count % 2:
                    ada_load(n0 + count - 1, (l, b0 + count - 1), (count - 1) % 2)
            ada_phase(0)
            for n in range(ADA_MIX[0], ADA_MIX[0] + ADA_MIX[1]):
                ada_load(n, (0, n), n % 2)
            ada_phase(1)
            ws_load(1)
            ada_phase(2)

        @block.scalar
        def _(act):
            nxt = [0]

            def split(chunk, slot, wait_slot=True):
                act.wait_ge(raw_landed[slot], 16 * (chunk // RING + 1))
                if wait_slot:
                    act.wait_ge(chunk_used, chunk - RING + 1)
                nc.scalar.activation(w_hi[:, slot, :], raw[:, slot, :], ACT.Copy).then_inc(hi_ready, 1)

            def split_at(base, step, i):
                c = base + i
                slot = c % RING
                act.wait_ge(raw_landed[slot], 16 * (c // RING + 1) + 16 * step)
                act.wait_ge(chunk_used, c - RING + 1 + RING * step)
                nc.scalar.activation(w_hi[:, slot, :], raw[:, slot, :], ACT.Copy).then_inc(hi_ready, 1)

            def advance(n):
                for _ in range(n):
                    if nxt[0] < ALL_CHUNKS:
                        split(nxt[0], nxt[0] % RING, nxt[0] >= RING)
                        nxt[0] += 1

            act.dma_start(rows_in[ROW_C:ROW_C + 8, 0, :], c.rearrange("o (k p) -> (o k) p", p=P)).then_inc(small_landed, 16)
            act.dma_start(rows_in[ROW_LB:ROW_NW, 0, :], lb_logits.rearrange("l (k p) -> (l k) p", p=P)).then_inc(small_landed, 16)
            act.dma_start(rows_in[ROW_NW:ROW_FN, 0, :], norm_w.rearrange("l s (k p) -> (l s k) p", p=P)).then_inc(small_landed, 16)
            act.dma_start(rows_in[ROW_FN:ROWS, 0, :], final_w.rearrange("(k p) -> k p", p=P)).then_inc(small_landed, 16)
            act.dma_start(rows_in[0:72, 1:3, :], ada_b.rearrange("l (k p) -> k l p", p=P)).then_inc(small_landed, 16)
            act.dma_start(ident[:, :], ident_in).then_inc(small_landed, 16)
            act.dma_start(x_in[:, :, :], x[0].rearrange("(n p) d -> p n d", p=P)).then_inc(x_landed, 16)
            act.dma_start(tril[:, :], tril_in).then_inc(const_landed, 16)
            act.dma_start(mask_in[:, :, :], level_mask_in).then_inc(const_landed, 16)
            act.sem_inc(gate_free, 2)

            act.wait_ge(params_ready, 2)
            nc.scalar.activation(c_act[:, :], params[:, ROW_C:ROW_C + KT], ACT.Silu).then_inc(c_ready, 1)
            act.wait_ge(softmax_v, 1)
            nc.scalar.activation(lb_t[:, 2:4, :], lb_t[:, 0:2, :], ACT.Exp).then_inc(softmax_a, 1)
            act.wait_ge(softmax_v, 2)
            nc.scalar.activation(lb_t[:, 5, :], lb_t[:, 4, :], ACT.Ln).then_inc(softmax_a, 1)
            for q in range(4):
                act.wait_ge(x_turned, q + 1)
                nc.scalar.activation(h[:, 2 * q:2 * q + 2, :].rearrange("p k t -> p (k t)"), bank[4 + q][:, :], ACT.Copy).then_inc(h_ready, 2)
            advance(4)

            def norm(n):
                for m in range(KT):
                    act.wait_ge(h_ready, KT * n + m + 1)
                    nc.scalar.activation(norm_tmp[:, m, :], h[:, m, :], ACT.Square).then_inc(sq_ready, 1)
                act.wait_ge(sum_ready, n + 1)
                nc.scalar.activation(rstd[:, :], norm_bank[n][:, 0:T], ACT.Sqrt, bias=eps_t[:, 0:1], scale=1.0 / D).then_inc(rms_ready, 1)
                if n == 3 * DEPTH:
                    return
                shift = (3 * n) * KT
                for m in range(KT):
                    act.wait_ge(t_ready, KT * n + m + 1)
                    nc.scalar.activation(x_hi[:, m, :], norm_tmp[:, m, :], ACT.Identity, bias=mod[:, shift + m:shift + m + 1]).then_inc(x_hi_ready, 1)

            def ffn(f):
                c0, j0 = ffn_chunk0(f), ffn_job0(f)
                n_split = nxt[0]

                def gate(p, parity):
                    act.wait_ge(chunk_used, c0 + 4 * p + 2)
                    act.wait_ge(up_free, PAIRS * f + p + 1)
                    nc.scalar.activation(silu_a[:, parity, :], job_bank(j0 + 2 * parity)[:, :], ACT.Silu).then_inc(gate_free, 1)
                    act.wait_ge(up_free, PAIRS * f + p + 3)
                    dst = g_hi[:, bass.ds(2 * p, 2), :] if not isinstance(p, int) else g_hi[:, 2 * p:2 * p + 2, :]
                    nc.scalar.activation(dst.rearrange("p k t -> p (k t)"), gated[:, parity, :], ACT.Copy).then_inc(g_hi_ready, 1)

                with act.Fori(0, PAIRS // 2) as t:
                    for parity in range(2):
                        for i in range(4):
                            split_at(n_split + 4 * parity, 2 * t, i)
                        gate(2 * t + parity, parity)
                nxt[0] += 8 * (PAIRS // 2)
                advance(4)
                gate(PAIRS - 1, 0)
                n_split = nxt[0]
                left = min(HT, ALL_CHUNKS - n_split)
                with act.Fori(0, left // 4) as t:
                    for i in range(4):
                        split_at(n_split, t, i)
                nxt[0] += left // 4 * 4
                advance(left % 4)

            def mixer(l):
                c0, j0 = mix_chunk0(l), mix_job0(l)

                def take(g, fn, dst, token_major=False, **kw):
                    for j in (2 * g, 2 * g + 1):
                        act.wait_ge(chunk_used, c0 + 2 * j + 2)
                        src, q = job_bank(j0 + j), j % 4
                        if token_major:
                            d = dst[:, :, :].rearrange("p k t -> p (k t)").rearrange("p (n d) -> p n d", n=NT)[:, :, q * JC:(q + 1) * JC]
                            s = src[:, :].rearrange("p (n d) -> p n d", n=NT)
                        else:
                            d = dst[:, 2 * q:2 * q + 2, :].rearrange("p k t -> p (k t)")
                            s = src[:, :]
                        nc.scalar.activation(d, s, fn, **kw).then_inc(proj_taken, 1)

                def level(n, m):
                    act.wait_ge(suffix_ready, 8 * l + n + 1)
                    d, pre = halves(decay, m), halves(logf, m)
                    nc.scalar.activation(d[:, :, 0, :], d[:, :, 0, :], ACT.Exp).then_inc(decay_ready, 1)
                    nc.scalar.activation(d[:, :, 1, :], pre[:, :, 1, :], ACT.Exp).then_inc(decay_ready, 1)

                steps = 3 if l == 0 else 6
                fa = [steps * 0 + (0 if l == 0 else 4)]
                fv = [l]

                def f_step(out_, in_, fn, wait_self=True, **kw):
                    if wait_self:
                        act.wait_ge(f_act, fa[0])
                    nc.scalar.activation(out_, in_, fn, **kw).then_inc(f_act, 1)
                    fa[0] += 1

                fl = logf[:, :, :].rearrange("p k t -> p (k t)")
                dl = decay[:, :, :].rearrange("p k t -> p (k t)")
                for g in (0, 1):
                    advance(4)
                    take(g, ACT.Copy, logf)
                act.wait_ge(proj_taken, PROJ_JOBS * l + 4)
                f_step(key[:, :, :].rearrange("p k t -> p (k t)"), fl, ACT.Sigmoid, False, scale=-1.0)
                f_step(dl, fl, ACT.Abs, False)
                f_step(dl, dl, ACT.Exp, scale=-1.0)
                f_step(dl, dl, ACT.Ln, bias=eps_t[:, 1:2])
                advance(4)
                take(2, ACT.Silu, query)
                if l > 0:
                    act.wait_ge(f_vec, fv[0] + 3)
                    f_step(dl, dl, ACT.Abs, False)
                    f_step(dl, dl, ACT.Exp, scale=-1.0)
                    f_step(dl, dl, ACT.Ln, bias=eps_t[:, 1:2])
                advance(4)
                take(3, ACT.Silu, query)
                advance(4)
                take(4, ACT.Gelu_apprx_tanh, v_gate, True)
                level(0, 1)
                advance(4)
                take(5, ACT.Gelu_apprx_tanh, v_gate, True)
                level(1, 2)
                advance(4)
                take(6, ACT.Gelu_apprx_tanh, u_gate)
                act.wait_ge(ln_var, l + 1)
                nc.scalar.activation(ln_rstd[:, :], ln_mv[:, :, 1], ACT.Sqrt, bias=eps_t[:, 0:1]).then_inc(ln_std, 1)
                level(2, 4)
                advance(4)
                take(7, ACT.Gelu_apprx_tanh, u_gate)
                level(3, 8)
                advance(4)
                take(8, ACT.Copy, val, True)
                level(4, 16)
                advance(4)
                take(9, ACT.Copy, val, True)
                act.wait_ge(mix_read, MIX_READS * l + 26)
                nc.scalar.activation(ya_hi[:, :, :].rearrange("p k t -> p (k t)"), u_gate[:, :, :].rearrange("p k t -> p (k t)"), ACT.Copy).then_inc(ya_hi_ready, 1)
                level(5, 32)
                advance(4)
                act.wait_ge(ya_lo_ready, l + 1)
                take(10, ACT.Sigmoid, og)
                level(6, 64)
                advance(4)
                take(11, ACT.Sigmoid, og)
                level(7, 128)
                advance(4)
                take(12, ACT.Sigmoid, ga)
                advance(4)
                take(13, ACT.Sigmoid, ga)
                for b in range(4):
                    act.wait_ge(o_done, 4 * l + b + 1)
                    nc.scalar.activation(o_t[:, 2 * b:2 * b + 2, :].rearrange("p k t -> p (k t)"), bank[b][:, :], ACT.Copy)
                    nc.scalar.activation(sq_o[:, 2 * b:2 * b + 2, :].rearrange("p k t -> p (k t)"), bank[b][:, :], ACT.Square).then_inc(o_taken, 1)
                advance(4)
                take(14, ACT.Sigmoid, gb)
                for b in range(4):
                    act.wait_ge(o_summed, 4 * l + b + 1)
                    r = rms_o[:, 2 * b:2 * b + 2, :].rearrange("p k t -> p (k t)")
                    nc.scalar.activation(r, bank[b][:, :], ACT.Ln, bias=eps_t[:, 0:1], scale=1.0 / P).then_inc(aa, 1)
                act.wait_ge(aa, 4 * (l + 1))
                rl = rms_o[:, :, :].rearrange("p k t -> p (k t)")
                nc.scalar.activation(rl, rl, ACT.Exp, scale=-0.5).then_inc(o_rms, 1)
                advance(4)
                take(15, ACT.Sigmoid, gb)
                advance(4)
                act.wait_ge(yb_full, l + 1)
                nc.scalar.activation(yb_hi[:, :, :].rearrange("p k t -> p (k t)"), o_t[:, :, :].rearrange("p k t -> p (k t)"), ACT.Copy).then_inc(yb_hi_ready, 1)
                advance(8)
                for b in range(4):
                    act.wait_ge(m_full, 4 * l + b + 1)
                    nc.scalar.activation(ya_hi[:, 2 * b:2 * b + 2, :].rearrange("p k t -> p (k t)"), ga[:, 2 * b:2 * b + 2, :].rearrange("p k t -> p (k t)"), ACT.Copy).then_inc(m_hi_ready, 1)
                    if b < 2:
                        advance(2)
                advance(8)

            for l in range(DEPTH):
                norm(3 * l)
                ffn(2 * l)
                norm(3 * l + 1)
                mixer(l)
                norm(3 * l + 2)
                ffn(2 * l + 1)
            norm(3 * DEPTH)
            for q in range(8):
                act.wait_ge(y_turned, q + 1)
                nc.scalar.activation(y_out[:, q // 4, (q % 4) * 256:(q % 4 + 1) * 256], bank[q][:, 0:256], ACT.Copy).then_inc(y_copied, 1)

        @block.vector
        def _(dve):
            nxt = [0]

            def low(c, slot, value):
                dve.wait_ge(hi_ready, value)
                nc.vector.tensor_tensor(w_lo[:, slot, :], raw[:, slot, :], w_hi[:, slot, :], ALU.subtract).then_inc(lo_ready, 1)

            def advance(n):
                for _ in range(n):
                    if nxt[0] < ALL_CHUNKS:
                        low(nxt[0], nxt[0] % RING, nxt[0] + 1)
                        nxt[0] += 1

            def flat(t):
                return t[:, :, :].rearrange("p k t -> p (k t)")

            chain = [0]

            def link(ins):
                chain[0] += 1
                ins.then_inc(vv, 1)
                dve.wait_ge(vv, chain[0])

            def ada_part(n, parity, acc, k):
                wk = ada_raw[:, parity, k, :]
                if k == 0:
                    last = nc.vector.tensor_scalar(acc, wk, c_act[:, 0:1], None, ALU.mult)
                else:
                    dve.wait_ge(ada_summed, KT * n + k)
                    last = nc.vector.scalar_tensor_tensor(out=acc, in0=wk, scalar=c_act[:, k:k + 1], in1=acc, op0=ALU.mult, op1=ALU.add)
                last.then_inc(ada_summed, 1)

            def ada_block(n, acc):
                dve.wait_ge(ada_landed[n % 2], 16 * (n // 2 + 1))
                for k in range(KT):
                    ada_part(n, n % 2, acc, k)

            nc.vector.memset(ones[:, :], 1.0).then_inc(ones_ready, 1)
            nc.vector.memset(eps_t[:, 0:1], EPS).then_inc(consts_ready, 1)
            nc.vector.memset(eps_t[:, 1:2], 1.0).then_inc(consts_ready, 1)
            dve.sem_inc(up_free, 2)
            dve.wait_ge(rows_turned, 1)
            nc.vector.tensor_copy(params[:, :], bank[1][:, 0:ROWS]).then_inc(params_ready, 1)
            nc.vector.tensor_copy(adab[:, :], bank[1][:, 128:128 + 144]).then_inc(params_ready, 1)
            dve.wait_ge(params_ready, 2)
            l0, l1 = params[:, ROW_LB:ROW_LB + 8], params[:, ROW_LB + 8:ROW_LB + 16]
            link(nc.vector.tensor_tensor(lb_t[:, 4, :], l0, l1, ALU.max))
            link(nc.vector.tensor_tensor(lb_t[:, 0, :], l0, lb_t[:, 4, :], ALU.subtract))
            nc.vector.tensor_tensor(lb_t[:, 1, :], l1, lb_t[:, 4, :], ALU.subtract).then_inc(softmax_v, 1)
            dve.wait_ge(softmax_a, 1)
            nc.vector.tensor_tensor(lb_t[:, 4, :], lb_t[:, 2, :], lb_t[:, 3, :], ALU.add).then_inc(softmax_v, 1)
            dve.wait_ge(softmax_a, 2)
            link(nc.vector.reciprocal(lb_t[:, 3, :], lb_t[:, 4, :]))
            link(nc.vector.tensor_tensor(lb_t[:, 0, :], lb_t[:, 0, :], lb_t[:, 5, :], ALU.subtract))
            link(nc.vector.tensor_tensor(lb_t[:, 1, :], lb_t[:, 1, :], lb_t[:, 5, :], ALU.subtract))
            link(nc.vector.tensor_tensor(lb_t[:, 2, :], lb_t[:, 2, :], lb_t[:, 3, :], ALU.mult))
            dve.wait_ge(const_landed, 32)
            nc.vector.tensor_copy(level_mask[:, :, :], mask_in[:, :, :])
            dve.wait_ge(c_ready, 1)

            for n in range(8):
                if n >= 2:
                    dve.wait_ge(ada_reduced, n - 1)
                ada_block(n, ada_acc[:, n % 2, :])
            dve.wait_ge(ada_reduced, 8)
            nc.vector.tensor_tensor(mod[:, 0:16], bank[0][:, 0:16], adab[:, 0:16], ALU.add).then_inc(mod_ready, 1)
            advance(4)

            mods = [1]

            def norm(n):
                final = n == 3 * DEPTH
                g = (3 * n) * KT
                if not final:
                    l, s = n // 3, n % 3
                    dve.wait_ge(mod_ready, mods[0])
                    nw = params[:, ROW_NW + 8 * n:ROW_NW + 8 * n + 8]
                    link(nc.vector.scalar_tensor_tensor(out=scale_a[:, :], in0=mod[:, g + KT:g + 2 * KT], scalar=1.0, in1=nw, op0=ALU.add, op1=ALU.mult))
                    scale = scale_a[:, :]
                else:
                    scale = params[:, ROW_FN:ROW_FN + 8]
                dve.wait_ge(rms_ready, n + 1)
                link(nc.vector.reciprocal(rstd[:, :], rstd[:, :]))

                def low_x(m):
                    dve.wait_ge(x_hi_ready, KT * n + m + 1)
                    nc.vector.scalar_tensor_tensor(out=x_lo[:, m, :], in0=norm_tmp[:, m, :], scalar=mod[:, g + m:g + m + 1], in1=x_hi[:, m, :], op0=ALU.add, op1=ALU.subtract).then_inc(x_lo_ready, 1)
                for m in range(KT):
                    dst = y_t if final else norm_tmp
                    nc.vector.scalar_tensor_tensor(out=dst[:, m, :], in0=h[:, m, :], scalar=scale[:, m:m + 1], in1=rstd[:, :], op0=ALU.mult, op1=ALU.mult).then_inc(y_ready if final else t_ready, 1)
                    if not final and m >= 2:
                        low_x(m - 2)
                if not final:
                    low_x(KT - 2)
                    low_x(KT - 1)

            def residual(n, factor, tile):
                g = (3 * (n - 1) + 2) * KT
                link(nc.vector.tensor_scalar(coef[:, :], mod[:, g:g + KT], 1.0, factor, ALU.add, ALU.mult))
                for m in range(KT):
                    src = tile(m)
                    nc.vector.scalar_tensor_tensor(out=h[:, m, :], in0=src, scalar=coef[:, m:m + 1], in1=h[:, m, :], op0=ALU.mult, op1=ALU.add).then_inc(h_ready, 1)

            def ffn(f):
                f0, j0 = ffn_chunk0(f), ffn_job0(f)
                n0, in_w13, per_loop, rest = ADA_PLAN[f]
                c0 = nxt[0]

                def up(p, parity):
                    dve.wait_ge(gate_free, PAIRS * f + p + 3)
                    dve.wait_ge(chunk_used, f0 + 4 * p + 4)
                    nc.vector.tensor_tensor(gated[:, parity, :], silu_a[:, parity, :], job_bank(j0 + 2 * parity + 1)[:, :], ALU.mult).then_inc(up_free, 1)
                    dve.wait_ge(g_hi_ready, PAIRS * f + p + 1)
                    k = slice(2 * p, 2 * p + 2) if isinstance(p, int) else bass.ds(2 * p, 2)
                    nc.vector.tensor_tensor(g_lo[:, k, :].rearrange("p k t -> p (k t)"), gated[:, parity, :], g_hi[:, k, :].rearrange("p k t -> p (k t)"), ALU.subtract).then_inc(g_lo_ready, 1)

                def ada_step(n, landed, parity, ks):
                    if ks[0] == 0:
                        dve.wait_ge(ada_landed[parity], landed)
                        dve.wait_ge(ada_reduced, n - 1)
                    for k in ks:
                        ada_part(n, parity, ada_acc[:, parity, :], k)

                def landed_count(n):
                    return 16 * (n // 2 + 1)

                with dve.Fori(0, PAIRS // 2) as t:
                    for parity in range(2):
                        for i in range(4):
                            if in_w13:
                                ada_step(n0 + 2 * t + parity, landed_count(n0 + parity) + 16 * t, parity, (2 * i, 2 * i + 1))
                            low(None, (c0 + i) % RING, c0 + 4 * parity + i + 1 + 8 * t)
                        up(2 * t + parity, parity)
                nxt[0] += 8 * (PAIRS // 2)
                if in_w13:
                    n = n0 + PAIRS - 1
                    for i in range(4):
                        ada_step(n, landed_count(n), 0, (2 * i, 2 * i + 1))
                        advance(1)
                else:
                    advance(4)
                up(PAIRS - 1, 0)
                if in_w13:
                    dve.wait_ge(ada_reduced, n0 + PAIRS)
                    a = 2 * n0
                    nc.vector.tensor_tensor(mod[:, a:a + 2 * PAIRS], bank[0][:, 0:2 * PAIRS], adab[:, a:a + 2 * PAIRS], ALU.add).then_inc(mod_ready, 1)
                    mods[0] += 1
                c0 = nxt[0]
                left = min(HT, ALL_CHUNKS - c0)
                n1 = n0 + PAIRS
                with dve.Fori(0, left // 4) as t:
                    for i in range(4):
                        if per_loop:
                            par = (n1 + i // 2) % 2
                            ada_step(n1 + 2 * t + i // 2, landed_count(n1 + i // 2) + 16 * t, par, range(4 * (i % 2), 4 * (i % 2) + 4))
                        low(None, (c0 + i) % RING, c0 + i + 1 + 4 * t)
                nxt[0] += left // 4 * 4
                advance(left % 4)
                n2 = n1 + 5 * per_loop
                for n in range(n2, n2 + rest):
                    ada_step(n, landed_count(n), n % 2, range(KT))
                if in_w13:
                    count = 5 * per_loop + rest
                    dve.wait_ge(ada_reduced, n1 + count)
                    a = 2 * n1
                    nc.vector.tensor_tensor(mod[:, a:a + 2 * count], bank[4][:, 0:2 * count], adab[:, a:a + 2 * count], ALU.add).then_inc(mod_ready, 1)
                    mods[0] += 1
                dve.wait_ge(mod_ready, mods[0])
                dve.wait_ge(chunk_used, f0 + FFN_CHUNKS)
                n = 3 * (f // 2) + 1 + 2 * (f % 2)
                residual(n, 0.5, lambda m: bank[m // 2][:, (m % 2) * T:(m % 2 + 1) * T])

            def mixer(l):
                c0, j0 = mix_chunk0(l), mix_job0(l)
                m0 = MIX_READS * l
                read = [m0]

                def wait_scored():
                    dve.wait_ge(mix_scored, read[0] + 1)
                    read[0] += 1

                fv = [l]

                dve.wait_ge(ws_landed, 16 * (l + 1))
                dve.wait_ge(const_landed, 32)
                nc.vector.tensor_tensor(ws_raw[:, :, :], ws_raw[:, :, :], tril[:, :].unsqueeze(1).to_broadcast([P, HEADS, P]), ALU.mult).then_inc(ws_masked, 1)
                advance(4)
                for b in range(2):
                    wait_scored()
                    nc.vector.tensor_copy(ws_t[:, 4 * b:4 * b + 4, :].rearrange("p g t -> p (g t)"), bank[b][:, :]).then_inc(mix_read, 1)
                advance(4)

                f0 = 0 if l == 0 else 4
                dl, fl = flat(decay), flat(logf)
                dve.wait_ge(f_act, f0 + 4)
                nc.vector.scalar_tensor_tensor(out=fl, in0=fl, scalar=0.0, in1=dl, op0=ALU.min, op1=ALU.subtract).then_inc(f_vec, 1)
                fv[0] += 1
                if l > 0:
                    def per_head(row):
                        return lb_t[:, row, :].unsqueeze(2).to_broadcast([P, HEADS, T])
                    dve.wait_ge(f_vec, fv[0])
                    nc.vector.tensor_tensor(logf[:, :, :], logf[:, :, :], per_head(0), ALU.add).then_inc(f_vec, 1)
                    fv[0] += 1
                    dve.wait_ge(f_vec, fv[0])
                    nc.vector.tensor_tensor(decay[:, :, :], logf[:, :, :], per_head(1), ALU.subtract).then_inc(f_vec, 1)
                    fv[0] += 1
                    nc.vector.tensor_tensor(logf[:, :, :], logf[:, :, :], per_head(1), ALU.max)
                    nc.vector.tensor_tensor(key[:, :, :], key[:, :, :], per_head(2), ALU.mult).then_inc(f_vec, 1)
                    fv[0] += 1
                    advance(2)
                    dve.wait_ge(f_act, f0 + 7)
                    dve.wait_ge(f_vec, fv[0])
                    nc.vector.tensor_tensor(logf[:, :, :], logf[:, :, :], decay[:, :, :], ALU.add).then_inc(f_vec, 1)
                    fv[0] += 1
                else:
                    advance(2)
                advance(2)

                def suffix(n, m):
                    pre, d = halves(logf, m), halves(decay, m)
                    mid = pre[:, :, 0, m - 1:m].to_broadcast([P, KT * T // (2 * m), m])
                    if n:
                        dve.wait_ge(vv, chain[0])
                    nc.vector.tensor_tensor(d[:, :, 0, :], mid, pre[:, :, 0, :], ALU.subtract).then_inc(suffix_ready, 1)

                def pairs(n, m):
                    pre, d, w = halves(logf, m), halves(decay, m), halves(pair, m)
                    dve.wait_ge(decay_ready, 16 * l + 2 * n + 2)
                    if n:
                        dve.wait_ge(mix_scored, read[0])
                    nc.vector.tensor_tensor(w[:, :, 0, :], halves(key, m)[:, :, 0, :], d[:, :, 0, :], ALU.mult)
                    nc.vector.tensor_tensor(w[:, :, 1, :], halves(query, m)[:, :, 1, :], d[:, :, 1, :], ALU.mult).then_inc(pair_ready, 1)
                    if m < P:
                        mid = pre[:, :, 0, m - 1:m].to_broadcast([P, KT * T // (2 * m), m])
                        chain[0] += 1
                        nc.vector.tensor_tensor(pre[:, :, 1, :], pre[:, :, 1, :], mid, ALU.add).then_inc(vv, 1)

                def merge(n):
                    for b in range(4):
                        wait_scored()
                        s = score[:, 2 * b:2 * b + 2, :].rearrange("p h (n t) -> p (h n) t", n=NT)
                        src = bank[b][:, :].rearrange("p (a t) -> p a t", t=P)
                        mask = level_mask[:, n, :].unsqueeze(1).to_broadcast([P, 4, P])
                        nc.vector.copy_predicated(s, mask, src).then_inc(mix_read, 1)

                dve.wait_ge(f_vec, fv[0])
                suffix(0, 1)
                advance(4)
                dve.wait_ge(proj_taken, PROJ_JOBS * l + 8)
                for b in range(4):
                    wait_scored()
                    s = score[:, 2 * b:2 * b + 2, :].rearrange("p h (n t) -> p (h n) t", n=NT)
                    src = bank[b][:, :].rearrange("p (a t) -> p a t", t=P)
                    nc.vector.tensor_tensor(s, src, ident[:, :].unsqueeze(1).to_broadcast([P, 4, P]), ALU.mult).then_inc(mix_read, 1)
                pairs(0, 1)
                suffix(1, 2)
                advance(4)
                merge(0)
                pairs(1, 2)
                suffix(2, 4)
                advance(4)
                merge(1)
                dve.wait_ge(proj_taken, PROJ_JOBS * l + 12)
                vt = v_gate[:, :, :].rearrange("p k t -> p (k t)").rearrange("p (a c) -> p a c", c=P)
                for a in range(16):
                    last = nc.vector.bn_stats(ln_stats[:, a, :], vt[:, a, :])
                link(last)
                for a in range(16):
                    last = nc.vector.bn_aggr(ln_mv[:, a, :], ln_stats[:, a, :])
                last.then_inc(ln_var, 1)
                advance(2)
                pairs(2, 4)
                suffix(3, 8)
                advance(2)
                dve.wait_ge(ln_std, l + 1)
                link(nc.vector.reciprocal(ln_rstd[:, :], ln_rstd[:, :]))
                for a in range(16):
                    last = nc.vector.tensor_scalar(vt[:, a, :], vt[:, a, :], ln_mv[:, a, 0:1], ln_rstd[:, a:a + 1], ALU.subtract, ALU.mult)
                last.then_inc(v_norm, 1)
                merge(2)
                advance(2)
                pairs(3, 8)
                suffix(4, 16)
                advance(2)
                merge(3)
                pairs(4, 16)
                suffix(5, 32)
                advance(4)
                for b in range(4):
                    wait_scored()
                    u = u_gate[:, 2 * b:2 * b + 2, :].rearrange("p k t -> p (k t)")
                    if b == 0:
                        dve.wait_ge(proj_taken, PROJ_JOBS * l + 16)
                    nc.vector.tensor_tensor(u, u, bank[b][:, :], ALU.mult).then_inc(mix_read, 1)
                advance(2)
                dve.wait_ge(ya_hi_ready, l + 1)
                nc.vector.tensor_tensor(flat(ya_lo), flat(u_gate), flat(ya_hi), ALU.subtract).then_inc(ya_lo_ready, 1)
                merge(4)
                pairs(5, 32)
                suffix(6, 64)
                advance(2)
                merge(5)
                advance(2)
                pairs(6, 64)
                suffix(7, 128)
                advance(2)
                merge(6)
                advance(2)
                pairs(7, 128)
                advance(2)
                for b in range(2):
                    wait_scored()
                    nc.vector.tensor_copy(decay[:, 2 * b:2 * b + 2, :].rearrange("p k t -> p (k t)"), bank[b][:, :]).then_inc(mix_read, 1)
                advance(4)
                if l == 0:
                    for n in range(ADA_MIX[0], ADA_MIX[0] + ADA_MIX[1]):
                        ada_block(n, ada_mix[:, n - ADA_MIX[0], :])
                        if n % 2:
                            advance(2)
                else:
                    advance(4)
                advance(4)
                dve.wait_ge(o_rms, l + 1)
                link(nc.vector.tensor_tensor(flat(o_t), flat(o_t), flat(rms_o), ALU.mult))
                advance(1)
                nc.vector.tensor_tensor(flat(o_t), flat(o_t), flat(og), ALU.mult).then_inc(yb_full, 1)
                advance(3)
                dve.wait_ge(yb_hi_ready, l + 1)
                nc.vector.tensor_tensor(flat(yb_lo), flat(o_t), flat(yb_hi), ALU.subtract).then_inc(yb_lo_ready, 1)
                advance(4)

                def branch(b, gate):
                    for q in range(4):
                        jj = 4 * b + q
                        dve.wait_ge(chunk_used, c0 + 64 + 2 * jj + 2)
                        g = gate[:, 2 * q:2 * q + 2, :].rearrange("p k t -> p (k t)")
                        if b == 0:
                            dve.wait_ge(proj_taken, PROJ_JOBS * (l + 1))
                        nc.vector.tensor_tensor(g, g, job_bank(j0 + PROJ_JOBS + jj)[:, :], ALU.mult).then_inc(branch_taken, 1)
                        if b == 1:
                            dve.wait_ge(branch_taken, 8 * l + jj + 1)
                            a = ga[:, 2 * q:2 * q + 2, :].rearrange("p k t -> p (k t)")
                            nc.vector.tensor_tensor(a, a, g, ALU.add).then_inc(m_full, 1)
                            dve.wait_ge(m_hi_ready, 4 * l + q + 1)
                            nc.vector.tensor_tensor(ya_lo[:, 2 * q:2 * q + 2, :].rearrange("p k t -> p (k t)"), a, ya_hi[:, 2 * q:2 * q + 2, :].rearrange("p k t -> p (k t)"), ALU.subtract).then_inc(m_lo_ready, 1)
                        if jj < 6:
                            advance(2)
                branch(0, ga)
                branch(1, gb)
                advance(8)
                if l == 0:
                    dve.wait_ge(ada_reduced, 36)
                    nc.vector.tensor_tensor(mod[:, 64:72], bank[0][:, 256:264], adab[:, 64:72], ALU.add).then_inc(mod_ready, 1)
                    mods[0] += 1
                    dve.wait_ge(mod_ready, mods[0])

                def tile(m):
                    jj = 8 + m // 2
                    if m % 2 == 0:
                        dve.wait_ge(chunk_used, c0 + 64 + 2 * jj + 2)
                    return job_bank(j0 + PROJ_JOBS + jj)[:, (m % 2) * T:(m % 2 + 1) * T]
                residual(3 * l + 2, 1.0, tile)

            for l in range(DEPTH):
                norm(3 * l)
                ffn(2 * l)
                norm(3 * l + 1)
                mixer(l)
                norm(3 * l + 2)
                ffn(2 * l + 1)
            norm(3 * DEPTH)

        @block.tensor
        def _(pe):
            def mm(out_, lhs, rhs, start, stop=False):
                return nc.tensor.matmul(out_, lhs, rhs, start=start, stop=stop, skip_group_check=True)

            def tiles(slot, k, m):
                at = k * JC + m * P
                return w_hi[:, slot, at:at + P], w_lo[:, slot, at:at + P]

            def three(out_, w, xs, start):
                (wh, wl), (xh, xl) = w, xs
                mm(out_, wh, xh, start)
                mm(out_, wh, xl, False)
                return mm(out_, wl, xh, False)

            def job(b, slot0, waits, src, token_major=False, ready=None):
                hi, lo = src
                for q in range(2):
                    slot = (slot0 + q) % RING
                    pe.wait_ge(lo_ready, waits[q])
                    for k in range(KC):
                        kk = KC * q + k
                        if ready is not None:
                            pe.wait_ge(ready[0], ready[1] + kk + 1)
                        for m in range(2):
                            start = kk == 0 and m == 0
                            dst = b[:, m * T:(m + 1) * T]
                            if token_major:
                                at = k * JC
                                whl = w_hi[:, slot, at:at + JC], w_lo[:, slot, at:at + JC]
                                xt = hi[:, kk, m * P:(m + 1) * P], lo[:, kk, m * P:(m + 1) * P]
                                mm(dst, xt[0], whl[0], start)
                                mm(dst, xt[0], whl[1], False)
                                last = mm(dst, xt[1], whl[0], False)
                            else:
                                last = three(dst, tiles(slot, k, m), (hi[:, kk, :], lo[:, kk, :]), start)
                    if q == 0:
                        last.then_inc(chunk_used, 1)
                return last

            def reduce_block(n, acc, dst):
                pe.wait_ge(ada_summed, KT * (n + 1))
                mm(dst[:, 0:1], acc[:, 0:P], ones[:, 0:1], True, True)
                mm(dst[:, 1:2], acc[:, P:2 * P], ones[:, 0:1], True, True).then_inc(ada_reduced, 1)

            pe.wait_ge(small_landed, 96)
            pe.wait_ge(ones_ready, 1)
            nc.tensor.transpose(bank[1][:, 0:ROWS], rows_in[0:ROWS, 0, :], ident[0:ROWS, 0:ROWS])
            for l in range(DEPTH):
                last = nc.tensor.transpose(bank[1][:, P + 72 * l:P + 72 * (l + 1)], rows_in[0:72, 1 + l, :], ident[0:72, 0:72])
            last.then_inc(rows_turned, 1)
            pe.wait_ge(x_landed, 16)
            for q in range(4):
                for i in range(4):
                    k, n = 2 * q + i // 2, i % 2
                    last = nc.tensor.transpose(bank[4 + q][:, i * P:(i + 1) * P], x_in[:, n, k * P:(k + 1) * P], ident[:, :])
                last.then_inc(x_turned, 1)
            for n in range(8):
                reduce_block(n, ada_acc[:, n % 2, :], bank[0][:, 2 * n:2 * n + 2])

            def norm(n):
                for m in range(KT):
                    pe.wait_ge(sq_ready, KT * n + m + 1)
                    last = mm(norm_bank[n][:, 0:T], ones[:, :], norm_tmp[:, m, :], m == 0, m == KT - 1)
                last.then_inc(sum_ready, 1)

            def ffn(f):
                c0, j0 = ffn_chunk0(f), ffn_job0(f)
                n0, in_w13, per_loop, rest = ADA_PLAN[f]
                n = 3 * (f // 2) + 2 * (f % 2)
                src = (x_hi, x_lo)
                pe.wait_ge(x_lo_ready, KT * (n + 1))

                def do_pair(p, parity):
                    for i, free in enumerate((gate_free, up_free)):
                        pe.wait_ge(free, PAIRS * f + p + 1)
                        at = c0 + 4 * p + 2 * i + 1
                        last = job(job_bank(j0 + 2 * parity + i), c0 + 2 * i, (at, at + 1), src)
                        last.then_inc(chunk_used, 1)
                    if in_w13:
                        reduce_at(n0 + p, parity, bank[0], 2 * p)

                def reduce_at(n_, parity, b, col):
                    pe.wait_ge(ada_summed, KT * n_ + KT)
                    acc = ada_acc[:, parity, :]
                    for m in range(2):
                        dst = b[:, bass.ds(col + m, 1)] if not isinstance(col, int) else b[:, col + m:col + m + 1]
                        last = mm(dst, acc[:, m * P:(m + 1) * P], ones[:, 0:1], True, True)
                    last.then_inc(ada_reduced, 1)

                with pe.Fori(0, PAIRS // 2) as t:
                    for parity in range(2):
                        do_pair(2 * t + parity, parity)
                do_pair(PAIRS - 1, 0)

                if in_w13:
                    pe.wait_ge(mod_ready, mod_count(f))
                d0 = c0 + 4 * PAIRS
                n1 = n0 + PAIRS

                def down(k, slot, first=False):
                    pe.wait_ge(lo_ready, d0 + k + 1)
                    pe.wait_ge(g_lo_ready, PAIRS * f + PAIRS)
                    ks = slice(k, k + 1) if isinstance(k, int) else bass.ds(k, 1)
                    hi = g_hi[:, ks, :].rearrange("p k t -> p (k t)")
                    lo = g_lo[:, ks, :].rearrange("p k t -> p (k t)")
                    for m in range(KT):
                        w = w_hi[:, slot, m * P:(m + 1) * P], w_lo[:, slot, m * P:(m + 1) * P]
                        last = three(bank[m // 2][:, (m % 2) * T:(m % 2 + 1) * T], w, (hi, lo), first and m % 2 == 0)
                    last.then_inc(chunk_used, 1)

                for k in range(2):
                    down(k, (d0 + k) % RING, k == 0)
                with pe.Fori(0, 5) as t:
                    for i in range(4):
                        down(4 * t + 2 + i, (d0 + 2 + i) % RING)
                        if per_loop and i % 2 == 1:
                            q = i // 2
                            reduce_at(n1 + 2 * t + q, (n1 + q) % 2, bank[4], 4 * t + 2 * q)
                n2 = n1 + 5 * per_loop
                for i in range(rest):
                    reduce_at(n2 + i, (n2 + i) % 2, bank[4], 2 * (5 * per_loop + i))

            def mod_count(f):
                return {0: 2, 1: 5, 2: 7}[f]

            def mixer(l):
                c0, j0 = mix_chunk0(l), mix_job0(l)
                m0 = MIX_READS * l
                done = [m0]
                src = (x_hi, x_lo)
                pe.wait_ge(x_lo_ready, KT * (3 * l + 2))

                def group(g, token_major=False):
                    for j in (2 * g, 2 * g + 1):
                        if j >= 4:
                            pe.wait_ge(proj_taken, PROJ_JOBS * l + j - 3)
                        at = c0 + 2 * j
                        last = job(job_bank(j0 + j), at, (at + 1, at + 2), src, token_major)
                        last.then_inc(chunk_used, 1)

                def wait_bank():
                    pe.wait_ge(mix_read, done[0] - 3)

                def scored(last):
                    last.then_inc(mix_scored, 1)
                    done[0] += 1

                def score_level(lhs, rhs):
                    for b in range(4):
                        if done[0] >= m0 + 6:
                            wait_bank()
                        for i in range(4):
                            hh, nn = 2 * b + i // 2, i % 2
                            last = mm(bank[b][:, i * P:(i + 1) * P], lhs[:, hh, nn * P:(nn + 1) * P], rhs[:, hh, nn * P:(nn + 1) * P], True, True)
                        scored(last)

                group(0)
                pe.wait_ge(ws_masked, l + 1)
                for b in range(2):
                    for i in range(4):
                        last = nc.tensor.transpose(bank[b][:, i * P:(i + 1) * P], ws_raw[:, 4 * b + i, :], ident[:, :])
                    scored(last)
                for g in (1, 2, 3):
                    group(g)
                pe.wait_ge(mix_read, m0 + 2)
                pe.wait_ge(proj_taken, PROJ_JOBS * l + 8)
                pe.wait_ge(f_vec, 1 if l == 0 else 6)
                score_level(key, query)
                for n in range(4):
                    group(4 + n, n < 2)
                    pe.wait_ge(pair_ready, 8 * l + n + 1)
                    score_level(pair, pair)
                group(8, True)
                pe.wait_ge(v_norm, l + 1)
                pe.wait_ge(bias_landed, 16 * (l + 1))
                vt = v_gate[:, :, :].rearrange("p k t -> p (k t)").rearrange("p (n g c) -> p n g c", n=NT, c=P)
                for b in range(4):
                    wait_bank()
                    for i in range(4):
                        g, nn = 2 * b + i // 2, i % 2
                        dst = bank[b][:, i * P:(i + 1) * P]
                        mm(dst, vt[:, nn, g, :], ws_t[:, g, :], True)
                        last = mm(dst, ones[0:1, :], bias_row[0:1, g, :], False, True)
                    scored(last)
                for n in range(4, 7):
                    if n == 4:
                        group(9, True)
                    else:
                        group(5 + n)
                    pe.wait_ge(pair_ready, 8 * l + n + 1)
                    score_level(pair, pair)
                group(12)
                pe.wait_ge(pair_ready, 8 * l + 8)
                for b in range(2):
                    wait_bank()
                    for i in range(4):
                        hh = 4 * b + i
                        last = mm(bank[b][:, i * P:(i + 1) * P], pair[:, hh, 0:P], pair[:, hh, P:2 * P], True, True)
                    scored(last)
                group(13)
                pe.wait_ge(mix_read, m0 + MIX_READS)
                vv_ = val[:, :, :].rearrange("p k t -> p (k t)").rearrange("p (n h c) -> p n h c", n=NT, c=P)
                cross = decay[:, 0:4, :].rearrange("p k (a t) -> p (k a) t", t=P)
                for b in range(4):
                    for i in range(4):
                        hh, nn = 2 * b + i // 2, i % 2
                        dst = bank[b][:, i * P:(i + 1) * P]
                        last = mm(dst, vv_[:, nn, hh, :], score[:, hh, nn * P:(nn + 1) * P], True, nn == 0)
                        if nn == 1:
                            last = mm(dst, vv_[:, 0, hh, :], cross[:, hh, :], False, True)
                    last.then_inc(o_done, 1)
                group(14)
                for b in range(4):
                    pe.wait_ge(o_taken, 4 * l + b + 1)
                    mm(bank[b][:, :], ones[:, :], sq_o[:, 2 * b:2 * b + 2, :].rearrange("p k t -> p (k t)"), True, True).then_inc(o_summed, 1)
                group(15)

                def out_jobs(b, operand, ready, per_tile):
                    for q in range(4):
                        jj = 4 * b + q
                        if jj < 4:
                            pe.wait_ge(proj_taken, PROJ_JOBS * l + PROJ_JOBS - 3 + jj)
                        else:
                            pe.wait_ge(branch_taken, 8 * l + jj - 3)
                        pe.wait_ge(ready, per_tile)
                        at = c0 + 64 + 2 * jj
                        job(job_bank(j0 + PROJ_JOBS + jj), at, (at + 1, at + 2), operand).then_inc(chunk_used, 1)
                out_jobs(0, (ya_hi, ya_lo), ya_lo_ready, l + 1)
                out_jobs(1, (yb_hi, yb_lo), yb_lo_ready, l + 1)
                if l == 0:
                    pe.wait_ge(o_rms, 1)
                    for i in range(ADA_MIX[1]):
                        reduce_block(ADA_MIX[0] + i, ada_mix[:, i, :], bank[0][:, 256 + 2 * i:258 + 2 * i])
                out_jobs(2, (ya_hi, ya_lo), m_lo_ready, 4 * (l + 1))

            for l in range(DEPTH):
                norm(3 * l)
                ffn(2 * l)
                norm(3 * l + 1)
                mixer(l)
                norm(3 * l + 2)
                ffn(2 * l + 1)
            norm(3 * DEPTH)
            for n in range(NT):
                for q in range(4):
                    for i in range(2):
                        k = 2 * q + i
                        pe.wait_ge(y_ready, k + 1)
                        last = nc.tensor.transpose(bank[4 * n + q][:, i * P:(i + 1) * P], y_t[:, k, n * P:(n + 1) * P], ident[:, :])
                    last.then_inc(y_turned, 1)


_INS = ['x', 'c', 'w_in', 'gmlp_ws', 'gmlp_b', 'hgrn_lb_logits', 'w_branch_a', 'w_branch_b', 'w_out',
        'ffn_w13', 'ffn_w2', 'norm_w', 'ada_w', 'ada_b', 'final_norm_w']


def _constants():
    i = np.arange(P)
    s, t = i[:, None], i[None, :]
    masks = [(s // (2 * m) == t // (2 * m)) & (s % (2 * m) < m) & (t % (2 * m) >= m) for m in LEVELS]
    return {
        'ident': np.eye(P, dtype=np.float32),
        'level_mask': np.ascontiguousarray(np.stack(masks, 1).astype(np.float32)),
        'tril': np.tril(np.ones((P, P), np.float32)),
    }


def kernel(**inputs):
    import concourse.bacc as _bacc
    from concourse.bass_utils import run_bass_kernel_spmd as _run

    nc = _bacc.Bacc("TRN2", target_bir_lowering=False, num_devices=1)
    arrays = {f"in_{n}": np.ascontiguousarray(inputs[n]) for n in _INS}
    arrays.update({f"const_{n}": a for n, a in _constants().items()})
    args = [nc.dram_tensor(n, a.shape, mybir.dt.from_np(a.dtype), kind="ExternalInput").ap() for n, a in arrays.items()]
    args.append(nc.dram_tensor("y", (1, T, D), F32, kind="ExternalOutput").ap())
    trunk(nc, *args)
    r = _run(nc, [arrays], core_ids=[0])
    return r.results[0]["y"]
```

```python
from contextlib import ExitStack

import numpy as np

import concourse.bass as bass
from concourse import mybir

F32 = mybir.dt.float32
F32R = mybir.dt.float32r
U8 = mybir.dt.uint8
ALU = mybir.AluOpType
ACT = mybir.ActivationFunctionType

P = 128
DEPTH = 2
D = 1024
T = 256
KT = D // P
NT = T // P
HID = 2816
HT = HID // P
EPS = 1e-6
HEADS = 8
N_ADA = 9

RING = 4
CHUNK = 1024
KC = 4
JC = 256
PAIRS = HID // JC
ADA_BLOCKS = N_ADA * D // 256

FFN_CHUNKS = 4 * PAIRS + HT
SEGMENTS = (3, 2, 1, 0, 4, 5, 6, 7)
GROUPS = 16
MIX_CHUNKS = 4 * GROUPS + 3 * 8
LAYER_CHUNKS = 2 * FFN_CHUNKS + MIX_CHUNKS
ALL_CHUNKS = DEPTH * LAYER_CHUNKS
FFN_JOBS = 2 * PAIRS
PROJ_JOBS = 2 * GROUPS
MIX_JOBS = PROJ_JOBS + 12
LAYER_JOBS = 2 * FFN_JOBS + MIX_JOBS

LEVELS = (1, 2, 4, 8, 16, 32, 64)
MIX_YA = 2 + 4 + 3 * 4 + 4
MIX_READS = 2 + 4 * (1 + len(LEVELS)) + 4 + 2
DOWN_LOOP = (HT - 2) // 4
EARLY = 8
ADA_PLAN = {0: (8, 5), 1: (32, 5), 2: (53, 2)}
ADA_MIX = {0: (29, 3), 1: (68, 4)}

ROW_C, ROW_LB, ROW_NW, ROW_FN, ROWS = 0, 8, 24, 72, 80


def trunk(nc, x, c, w_in, gmlp_ws, gmlp_b, lb_logits, w_a, w_b, w_o, w13, w2, norm_w, ada_w, ada_b,
          final_w, ident_in, level_mask_in, tril_in, out):
    ctx = ExitStack()
    with ctx:
        def sb(name, shape, dt=F32, stack=ctx):
            return stack.enter_context(nc.sbuf_tensor(name, shape, dt))

        def sem(name):
            return ctx.enter_context(nc.semaphore(name))

        raw = sb("raw", [P, RING, CHUNK])
        w_hi = sb("w_hi", [P, RING, CHUNK], F32R)
        w_lo = sb("w_lo", [P, RING, CHUNK], F32R)
        ada_raw = sb("ada_raw", [P, 2, KT, 256])
        ada_acc = sb("ada_acc", [P, 2, 256])
        ada_mix = sb("ada_mix", [P, 4, 256])
        h = sb("h", [P, KT, T])
        x_hi = sb("x_hi", [P, KT, T], F32R)
        x_lo = sb("x_lo", [P, KT, T], F32R)
        mod = sb("mod", [P, DEPTH * N_ADA * KT])
        params = sb("params", [P, ROWS])
        adab = sb("adab", [P, DEPTH * N_ADA * KT])
        c_act = sb("c_act", [P, KT])
        scale_a = sb("scale_a", [P, KT])
        coef = sb("coef", [P, KT])
        rstd = sb("rstd", [P, T])
        ones = sb("ones", [P, P])
        act_scratch = sb("act_scratch", [P, 1])
        eps_t = sb("eps_t", [P, 2])
        ident = sb("ident", [P, P])
        tril = sb("tril", [P, P])
        level_mask = sb("level_mask", [P, len(LEVELS), P], U8)
        lb_t = sb("lb_t", [P, 6, HEADS])
        bias_row = sb("bias_row", [1, HEADS, P])
        ln_stats = sb("ln_stats", [P, 16, 6])
        ln_mv = sb("ln_mv", [P, 16, 2])
        ln_rstd = sb("ln_rstd", [P, 16])
        ws_t = sb("ws_t", [P, HEADS, P])

        with ExitStack() as tmp:
            silu_a = sb("silu_a", [P, 2, 512], F32, tmp)
            gated = sb("gated", [P, 2, 512], F32, tmp)
        norm_tmp = sb("norm_tmp", [P, KT, T])

        with ExitStack() as tmp:
            g_hi = sb("g_hi", [P, HT, T], F32R, tmp)
            g_lo = sb("g_lo", [P, HT, T], F32R, tmp)
        def unit(name, dt=F32, stack=ctx):
            return sb(name, [P, KT, T], dt, stack)
        with ExitStack() as tmp:
            rows_in = sb("rows_in", [P, 3, P], F32, tmp)
            x_in = sb("x_in", [P, NT, D], F32, tmp)
            mask_in = sb("mask_in", [P, len(LEVELS), P], F32, tmp)
            y_out = sb("y_out", [P, NT, D], F32, tmp)
            y_t = sb("y_t", [P, KT, T], F32, tmp)
            ada_early = sb("ada_early", [P, EARLY - 2, KT, 256], F32, tmp)
        with ExitStack() as tmp:
            yb_hi = unit("yb_hi", F32R, tmp)
            yb_lo = unit("yb_lo", F32R, tmp)
        key = unit("key")
        query = unit("query")
        logf = unit("logf")
        pair = unit("pair")
        decay = unit("decay")
        score = unit("score")
        val = unit("val")
        with ExitStack() as tmp:
            v_gate = unit("v_gate", F32, tmp)
        ya_hi = unit("ya_hi", F32R)
        u_gate = unit("u_gate")
        ya_lo = unit("ya_lo", F32R)
        ga = unit("ga")
        ws_raw = sb("ws_raw", [P, HEADS, P])
        o_t, gb, og = logf, pair, u_gate
        sq_o, rms_o = key, query

        bank = [ctx.enter_context(nc.psum_tensor(f"bank{i}", [P, 512], F32)) for i in range(8)]

        raw_landed = [sem(f"raw_landed{i}") for i in range(RING)]
        hi_ready, lo_ready, chunk_used = (sem(n) for n in ("hi_ready", "lo_ready", "chunk_used"))
        gate_free, up_free = sem("gate_free"), sem("up_free")
        g_hi_ready, g_lo_ready = sem("g_hi_ready"), sem("g_lo_ready")
        proj_taken, branch_taken = sem("proj_taken"), sem("branch_taken")
        small_landed, x_landed, const_landed = sem("small_landed"), sem("x_landed"), sem("const_landed")
        ws_landed, bias_landed = sem("ws_landed"), sem("bias_landed")
        ones_ready, consts_ready, setup_v = sem("ones_ready"), sem("consts_ready"), sem("setup_v")
        rows_turned, params_ready, c_ready = sem("rows_turned"), sem("params_ready"), sem("c_ready")
        x_turned, h_loaded = sem("x_turned"), sem("h_loaded")
        early_landed = [sem(f"early_landed{i}") for i in range(EARLY)]
        ada_landed = [sem("ada_landed0"), sem("ada_landed1")]
        down_done = sem("down_done")
        ada_summed, ada_reduced, mod_ready = sem("ada_summed"), sem("ada_reduced"), sem("mod_ready")
        h_ready, sq_ready, sum_ready, rms_ready = sem("h_ready"), sem("sq_ready"), sem("sum_ready"), sem("rms_ready")
        t_ready, x_hi_ready, x_lo_ready, vv = sem("t_ready"), sem("x_hi_ready"), sem("x_lo_ready"), sem("vv")
        aa = sem("aa")
        softmax_v, softmax_a = sem("softmax_v"), sem("softmax_a")
        ws_masked, mix_scored, mix_read = sem("ws_masked"), sem("mix_scored"), sem("mix_read")
        f_act, f_vec = sem("f_act"), sem("f_vec")
        suffix_ready, decay_ready, pair_ready = sem("suffix_ready"), sem("decay_ready"), sem("pair_ready")
        ln_var, ln_std, v_norm = sem("ln_var"), sem("ln_std"), sem("v_norm")
        ya_hi_ready, ya_lo_ready = sem("ya_hi_ready"), sem("ya_lo_ready")
        o_done, o_taken, o_summed, o_rms = sem("o_done"), sem("o_taken"), sem("o_summed"), sem("o_rms")
        yb_full, yb_hi_ready, yb_lo_ready = sem("yb_full"), sem("yb_hi_ready"), sem("yb_lo_ready")
        m_full, m_hi_ready, m_lo_ready = sem("m_full"), sem("m_hi_ready"), sem("m_lo_ready")
        y_ready, y_turned, y_copied, y_stored = sem("y_ready"), sem("y_turned"), sem("y_copied"), sem("y_stored")

        def ffn_chunk0(f):
            return (f // 2) * LAYER_CHUNKS + (f % 2) * (FFN_CHUNKS + MIX_CHUNKS)

        def ffn_job0(f):
            return (f // 2) * LAYER_JOBS + (f % 2) * (FFN_JOBS + MIX_JOBS)

        def mix_chunk0(l):
            return l * LAYER_CHUNKS + FFN_CHUNKS

        def mix_job0(l):
            return l * LAYER_JOBS + FFN_JOBS

        def job_bank(j):
            return bank[4 + j % 4]

        norm_bank = {0: bank[2], 1: bank[7], 2: bank[0], 3: bank[7], 4: bank[7], 5: bank[0], 6: bank[7]}

        def landed_count(n):
            return 16 * (n // 2 - EARLY // 2 + 1)

        def ada_plan(f):
            return (ADA_PLAN[f][0], PAIRS, ADA_PLAN[f][1]) if f in ADA_PLAN else (None, 0, 0)

        def halves(t, m):
            flat = t[:, :, :].rearrange("p h t -> p (h t)")
            return flat.rearrange("p (b two m) -> p b two m", two=2, m=m)

        block = ctx.enter_context(nc.Block())

        w13_v = w13.rearrange("l w (q k p) c -> l w q p k c", k=KC, p=P)
        w2_v = w2.rearrange("l w (k p) c -> l w p k c", p=P)
        ada_v = ada_w.rearrange("l (k p) c -> l p k c", p=P)
        in_v = w_in.rearrange("l (q k p) c -> l q p k c", k=KC, p=P)
        mix_v = [w.rearrange("l (q k p) c -> l q p k c", k=KC, p=P) for w in (w_a, w_b, w_o)]

        @block.sync
        def _(sp):
            def load(slot, src, wait):
                if wait is not None:
                    sp.wait_ge(lo_ready, wait)
                dst = raw[:, slot, :]
                if len(src.shape) == 3:
                    dst = dst.rearrange("p (k c) -> p k c", k=KC)
                sp.dma_start(dst, src).then_inc(raw_landed[slot], 16)

            def ffn(f):
                l, w, c0 = f // 2, f % 2, ffn_chunk0(f)

                def pair_loads(p, first):
                    for i in range(4):
                        col = p * JC + (i // 2) * HID
                        load((c0 + i) % RING, w13_v[l, w, i % 2][:, :, bass.ds(col, JC)],
                             None if first else c0 + 4 * p + i - RING + 1)
                if f == 0:
                    pair_loads(0, True)
                    with sp.Fori(1, PAIRS) as p:
                        pair_loads(p, False)
                else:
                    with sp.Fori(0, PAIRS) as p:
                        pair_loads(p, False)
                d0 = c0 + 4 * PAIRS
                with sp.Fori(0, HT // 4) as t:
                    for i in range(4):
                        load((d0 + i) % RING, w2_v[l, w][:, bass.ds(4 * t + i, 1), :].rearrange("p k c -> p (k c)"),
                             d0 + 4 * t + i - RING + 1)
                for k in range(HT // 4 * 4, HT):
                    load((d0 + k) % RING, w2_v[l, w][:, k, :], d0 + k - RING + 1)

            def mixer(l):
                c0 = mix_chunk0(l)
                for half in range(2):
                    with sp.Fori(0, 4) as s:
                        first = s * D + 4 * D if half else s * -D + 3 * D
                        for i in range(8):
                            at = c0 + 32 * half + i
                            load(at % RING, in_v[l, i % 2][:, :, bass.ds(first + (i // 2) * JC, JC)],
                                 at + 8 * s - RING + 1)
                for b in range(3):
                    for i in range(8):
                        at = c0 + 64 + 8 * b + i
                        load(at % RING, mix_v[b][l, i % 2][:, :, (i // 2) * JC:(i // 2 + 1) * JC], at - RING + 1)

            for n in range(EARLY):
                dst = ada_early[:, n, :, :] if n < EARLY - 2 else ada_raw[:, n % 2, :, :]
                sp.dma_start(dst, ada_v[0][:, :, n * 256:(n + 1) * 256]).then_inc(early_landed[n], 16)
            for l in range(DEPTH):
                ffn(2 * l)
                mixer(l)
                ffn(2 * l + 1)
            for n in range(NT):
                sp.wait_ge(y_copied, 4 * (n + 1))
                sp.dma_start(out[0, n * P:(n + 1) * P, :], y_out[:, n, :]).then_inc(y_stored, 16)
            sp.wait_ge(y_stored, 16 * NT)

        @block.gpsimd
        def _(pool):
            def ada_load(n, blk, parity):
                pool.wait_ge(ada_summed, KT * n - KT)
                l, b = blk
                pool.dma_start(ada_raw[:, parity, :, :], ada_v[l][:, :, bass.ds(b * 256, 256)]).then_inc(ada_landed[parity], 16)

            def ws_load(l):
                if l:
                    pool.wait_ge(mix_read, MIX_READS * l)
                    pool.wait_ge(mix_scored, MIX_READS * l)
                pool.dma_start(ws_raw[:, :, :], gmlp_ws[l].rearrange("g t s -> t g s")).then_inc(ws_landed, 16)
                pool.dma_start(bias_row[:, :, :], gmlp_b[l:l + 1]).then_inc(bias_landed, 16)

            def run(n0, count):
                l, b0 = n0 // ADA_BLOCKS, n0 % ADA_BLOCKS
                with pool.Fori(0, count // 2) as t:
                    for i in range(2):
                        ada_load(n0 + 2 * t + i, (l, b0 + 2 * t + i), (n0 + i) % 2)
                if count % 2:
                    ada_load(n0 + count - 1, (l, b0 + count - 1), (n0 + count - 1) % 2)

            ws_load(0)
            run(EARLY, ADA_BLOCKS - EARLY)
            last = ADA_PLAN[2][0]
            run(ADA_BLOCKS, last - ADA_BLOCKS)
            ws_load(1)
            run(last, 2 * ADA_BLOCKS - last)

        @block.scalar
        def _(act):
            nxt = [0]

            def split(chunk, slot, wait_slot=True):
                act.wait_ge(raw_landed[slot], 16 * (chunk // RING + 1))
                if wait_slot:
                    act.wait_ge(chunk_used, chunk - RING + 1)
                nc.scalar.activation(w_hi[:, slot, :], raw[:, slot, :], ACT.Copy).then_inc(hi_ready, 1)

            def split_at(base, step, i):
                c = base + i
                slot = c % RING
                act.wait_ge(raw_landed[slot], 16 * (c // RING + 1) + 16 * step)
                act.wait_ge(chunk_used, c - RING + 1 + RING * step)
                nc.scalar.activation(w_hi[:, slot, :], raw[:, slot, :], ACT.Copy).then_inc(hi_ready, 1)

            def advance(n):
                for _ in range(n):
                    if nxt[0] < ALL_CHUNKS:
                        split(nxt[0], nxt[0] % RING, nxt[0] >= RING)
                        nxt[0] += 1

            act.dma_start(rows_in[ROW_C:ROW_C + 8, 0, :], c.rearrange("o (k p) -> (o k) p", p=P)).then_inc(small_landed, 16)
            act.dma_start(rows_in[ROW_LB:ROW_NW, 0, :], lb_logits.rearrange("l (k p) -> (l k) p", p=P)).then_inc(small_landed, 16)
            act.dma_start(rows_in[ROW_NW:ROW_FN, 0, :], norm_w.rearrange("l s (k p) -> (l s k) p", p=P)).then_inc(small_landed, 16)
            act.dma_start(rows_in[ROW_FN:ROWS, 0, :], final_w.rearrange("(k p) -> k p", p=P)).then_inc(small_landed, 16)
            act.dma_start(rows_in[0:72, 1:3, :], ada_b.rearrange("l (k p) -> k l p", p=P)).then_inc(small_landed, 16)
            act.dma_start(ident[:, :], ident_in).then_inc(small_landed, 16)
            act.dma_start(x_in[:, :, :], x[0].rearrange("(n p) d -> p n d", p=P)).then_inc(x_landed, 16)
            act.dma_start(tril[:, :], tril_in).then_inc(const_landed, 16)
            act.dma_start(mask_in[:, :, :], level_mask_in).then_inc(const_landed, 16)
            act.sem_inc(gate_free, 2)

            act.wait_ge(params_ready, 2)
            nc.scalar.activation(c_act[:, :], params[:, ROW_C:ROW_C + KT], ACT.Silu).then_inc(c_ready, 1)
            act.wait_ge(softmax_v, 1)
            nc.scalar.activation(lb_t[:, 2:4, :], lb_t[:, 0:2, :], ACT.Exp).then_inc(softmax_a, 1)
            act.wait_ge(softmax_v, 2)
            nc.scalar.activation(lb_t[:, 5, :], lb_t[:, 4, :], ACT.Ln).then_inc(softmax_a, 1)
            for q in range(4):
                act.wait_ge(x_turned, q + 1)
                nc.scalar.activation(h[:, 2 * q:2 * q + 2, :].rearrange("p k t -> p (k t)"), bank[4 + q][:, :], ACT.Copy).then_inc(h_ready, 2)

            def norm(n):
                nc.scalar.activation(act_scratch[:, :], eps_t[:, 0:1], ACT.Sqrt)
                for m in range(KT):
                    if n % 3 == 2 and m and m % 2 == 0:
                        advance(2)
                    act.wait_ge(h_ready, KT * n + m + 1)
                    nc.scalar.activation(norm_tmp[:, m, :], h[:, m, :], ACT.Square).then_inc(sq_ready, 1)
                if n:
                    advance(1)
                act.wait_ge(sum_ready, n + 1)
                nc.scalar.activation(rstd[:, :], norm_bank[n][:, 0:T], ACT.Sqrt, bias=eps_t[:, 0:1], scale=1.0 / D).then_inc(rms_ready, 1)
                if n == 3 * DEPTH:
                    return
                advance(1 if n else 2)
                shift = (3 * n) * KT
                for m in range(KT):
                    act.wait_ge(t_ready, KT * n + m + 1)
                    nc.scalar.activation(x_hi[:, m, :], norm_tmp[:, m, :], ACT.Identity, bias=mod[:, shift + m:shift + m + 1]).then_inc(x_hi_ready, 1)
                if n == 0:
                    advance(2)

            def ffn(f):
                c0, j0 = ffn_chunk0(f), ffn_job0(f)
                n_split = nxt[0]

                def gate(p, parity):
                    act.wait_ge(chunk_used, c0 + 4 * p + 2)
                    act.wait_ge(up_free, PAIRS * f + p + 1)
                    nc.scalar.activation(silu_a[:, parity, :], job_bank(j0 + 2 * parity)[:, :], ACT.Silu).then_inc(gate_free, 1)
                    act.wait_ge(up_free, PAIRS * f + p + 3)
                    dst = g_hi[:, bass.ds(2 * p, 2), :] if not isinstance(p, int) else g_hi[:, 2 * p:2 * p + 2, :]
                    nc.scalar.activation(dst.rearrange("p k t -> p (k t)"), gated[:, parity, :], ACT.Copy).then_inc(g_hi_ready, 1)

                with act.Fori(0, PAIRS // 2) as t:
                    for parity in range(2):
                        for i in range(4):
                            split_at(n_split + 4 * parity, 2 * t, i)
                        gate(2 * t + parity, parity)
                nxt[0] += 8 * (PAIRS // 2)
                advance(4)
                gate(PAIRS - 1, 0)
                n_split = nxt[0]
                steps = min(DOWN_LOOP, (ALL_CHUNKS - n_split) // 4)
                with act.Fori(0, steps) as t:
                    for i in range(4):
                        split_at(n_split, t, i)
                nxt[0] += 4 * steps
                if steps < DOWN_LOOP:
                    advance(2)

            def mixer(l):
                c0, j0 = mix_chunk0(l), mix_job0(l)

                def take(g, fn, dst, token_major=False, **kw):
                    for j in (2 * g, 2 * g + 1):
                        act.wait_ge(chunk_used, c0 + 2 * j + 2)
                        src, q = job_bank(j0 + j), j % 4
                        if token_major:
                            d = dst[:, :, :].rearrange("p k t -> p (k t)").rearrange("p (n d) -> p n d", n=NT)[:, :, q * JC:(q + 1) * JC]
                            s = src[:, :].rearrange("p (n d) -> p n d", n=NT)
                        else:
                            d = dst[:, 2 * q:2 * q + 2, :].rearrange("p k t -> p (k t)")
                            s = src[:, :]
                        nc.scalar.activation(d, s, fn, **kw).then_inc(proj_taken, 1)

                def level(n, m):
                    act.wait_ge(suffix_ready, 8 * l + n + 1)
                    d, pre = halves(decay, m), halves(logf, m)
                    nc.scalar.activation(d[:, :, 0, :], d[:, :, 0, :], ACT.Exp).then_inc(decay_ready, 1)
                    nc.scalar.activation(d[:, :, 1, :], pre[:, :, 1, :], ACT.Exp).then_inc(decay_ready, 1)

                steps = 3 if l == 0 else 6
                fa = [steps * 0 + (0 if l == 0 else 4)]
                fv = [l]

                def f_step(out_, in_, fn, wait_self=True, **kw):
                    if wait_self:
                        act.wait_ge(f_act, fa[0])
                    nc.scalar.activation(out_, in_, fn, **kw).then_inc(f_act, 1)
                    fa[0] += 1

                fl = logf[:, :, :].rearrange("p k t -> p (k t)")
                dl = decay[:, :, :].rearrange("p k t -> p (k t)")
                advance(4)
                take(0, ACT.Copy, logf)
                advance(4)
                take(1, ACT.Copy, logf)
                act.wait_ge(proj_taken, PROJ_JOBS * l + 4)
                f_step(key[:, :, :].rearrange("p k t -> p (k t)"), fl, ACT.Sigmoid, False, scale=-1.0)
                advance(1)
                f_step(dl, fl, ACT.Abs, False)
                advance(1)
                f_step(dl, dl, ACT.Exp, scale=-1.0)
                advance(2)
                f_step(dl, dl, ACT.Ln, bias=eps_t[:, 1:2])
                take(2, ACT.Silu, query)
                advance(2)
                if l > 0:
                    act.wait_ge(f_vec, fv[0] + 3)
                    f_step(dl, dl, ACT.Abs, False)
                    advance(1)
                    f_step(dl, dl, ACT.Exp, scale=-1.0)
                    advance(1)
                    f_step(dl, dl, ACT.Ln, bias=eps_t[:, 1:2])
                else:
                    advance(2)
                take(3, ACT.Silu, query)

                def step(g, n, *taken, **kw):
                    advance(2)
                    if n is not None:
                        level(n, 2 ** n)
                    advance(2)
                    if taken:
                        take(g, *taken, **kw)
                step(4, 0, ACT.Gelu_apprx_tanh, v_gate, token_major=True)
                step(5, 1, ACT.Gelu_apprx_tanh, v_gate, token_major=True)
                step(6, 2, ACT.Gelu_apprx_tanh, u_gate)
                step(7, None, ACT.Gelu_apprx_tanh, u_gate)
                act.wait_ge(ln_var, l + 1)
                nc.scalar.activation(ln_rstd[:, :], ln_mv[:, :, 1], ACT.Sqrt, bias=eps_t[:, 0:1]).then_inc(ln_std, 1)
                step(8, 3, ACT.Copy, val, token_major=True)
                step(9, 4)
                act.wait_ge(mix_read, MIX_READS * l + MIX_YA)
                nc.scalar.activation(ya_hi[:, :, :].rearrange("p k t -> p (k t)"), u_gate[:, :, :].rearrange("p k t -> p (k t)"), ACT.Copy).then_inc(ya_hi_ready, 1)
                take(9, ACT.Copy, val, True)
                step(10, 5)
                act.wait_ge(ya_lo_ready, l + 1)
                take(10, ACT.Sigmoid, og)
                step(11, 6, ACT.Sigmoid, og)
                step(12, 7, ACT.Sigmoid, ga)
                step(13, None, ACT.Sigmoid, ga)
                step(14, None, ACT.Sigmoid, gb)
                for b in range(4):
                    act.wait_ge(o_done, 4 * l + b + 1)
                    nc.scalar.activation(o_t[:, 2 * b:2 * b + 2, :].rearrange("p k t -> p (k t)"), bank[b][:, :], ACT.Copy)
                    nc.scalar.activation(sq_o[:, 2 * b:2 * b + 2, :].rearrange("p k t -> p (k t)"), bank[b][:, :], ACT.Square).then_inc(o_taken, 1)
                step(15, None, ACT.Sigmoid, gb)
                for b in range(4):
                    act.wait_ge(o_summed, 4 * l + b + 1)
                    r = rms_o[:, 2 * b:2 * b + 2, :].rearrange("p k t -> p (k t)")
                    nc.scalar.activation(r, bank[b][:, :], ACT.Ln, bias=eps_t[:, 0:1], scale=1.0 / P).then_inc(aa, 1)
                act.wait_ge(aa, 4 * (l + 1))
                rl = rms_o[:, :, :].rearrange("p k t -> p (k t)")
                nc.scalar.activation(rl, rl, ACT.Exp, scale=-0.5).then_inc(o_rms, 1)
                advance(2)
                act.wait_ge(yb_full, l + 1)
                nc.scalar.activation(yb_hi[:, :, :].rearrange("p k t -> p (k t)"), o_t[:, :, :].rearrange("p k t -> p (k t)"), ACT.Copy).then_inc(yb_hi_ready, 1)
                advance(6)
                for b in range(4):
                    if b < 3:
                        advance(2)
                    act.wait_ge(m_full, 4 * l + b + 1)
                    nc.scalar.activation(ya_hi[:, 2 * b:2 * b + 2, :].rearrange("p k t -> p (k t)"), ga[:, 2 * b:2 * b + 2, :].rearrange("p k t -> p (k t)"), ACT.Copy).then_inc(m_hi_ready, 1)
                advance(2)

            for l in range(DEPTH):
                norm(3 * l)
                ffn(2 * l)
                norm(3 * l + 1)
                mixer(l)
                norm(3 * l + 2)
                ffn(2 * l + 1)
            norm(3 * DEPTH)
            for q in range(8):
                act.wait_ge(y_turned, q + 1)
                nc.scalar.activation(y_out[:, q // 4, (q % 4) * 256:(q % 4 + 1) * 256], bank[q][:, 0:256], ACT.Copy).then_inc(y_copied, 1)

        @block.vector
        def _(dve):
            nxt = [0]

            def low(c, slot, value):
                dve.wait_ge(hi_ready, value)
                nc.vector.tensor_tensor(w_lo[:, slot, :], raw[:, slot, :], w_hi[:, slot, :], ALU.subtract).then_inc(lo_ready, 1)

            def advance(n):
                for _ in range(n):
                    if nxt[0] < ALL_CHUNKS:
                        low(nxt[0], nxt[0] % RING, nxt[0] + 1)
                        nxt[0] += 1

            def flat(t):
                return t[:, :, :].rearrange("p k t -> p (k t)")

            chain = [0]

            def link(ins):
                chain[0] += 1
                ins.then_inc(vv, 1)
                dve.wait_ge(vv, chain[0])

            def ada_part(n, block_in, acc, k):
                wk = block_in[:, k, :]
                if k == 0:
                    last = nc.vector.tensor_scalar(acc, wk, c_act[:, 0:1], None, ALU.mult)
                else:
                    dve.wait_ge(ada_summed, KT * n + k)
                    last = nc.vector.scalar_tensor_tensor(out=acc, in0=wk, scalar=c_act[:, k:k + 1], in1=acc, op0=ALU.mult, op1=ALU.add)
                last.then_inc(ada_summed, 1)

            def ada_block(n, acc):
                dve.wait_ge(ada_landed[n % 2], landed_count(n))
                for k in range(KT):
                    ada_part(n, ada_raw[:, n % 2, :, :], acc, k)

            nc.vector.memset(ones[:, :], 1.0).then_inc(ones_ready, 1)
            nc.vector.memset(eps_t[:, 0:1], EPS).then_inc(consts_ready, 1)
            nc.vector.memset(eps_t[:, 1:2], 1.0).then_inc(consts_ready, 1)
            dve.sem_inc(up_free, 2)
            dve.wait_ge(rows_turned, 1)
            nc.vector.tensor_copy(params[:, :], bank[1][:, 0:ROWS]).then_inc(params_ready, 1)
            nc.vector.tensor_copy(adab[:, :], bank[1][:, 128:128 + 144]).then_inc(params_ready, 1)
            dve.wait_ge(params_ready, 2)
            l0, l1 = params[:, ROW_LB:ROW_LB + 8], params[:, ROW_LB + 8:ROW_LB + 16]
            link(nc.vector.tensor_tensor(lb_t[:, 4, :], l0, l1, ALU.max))
            link(nc.vector.tensor_tensor(lb_t[:, 0, :], l0, lb_t[:, 4, :], ALU.subtract))
            nc.vector.tensor_tensor(lb_t[:, 1, :], l1, lb_t[:, 4, :], ALU.subtract).then_inc(softmax_v, 1)
            dve.wait_ge(softmax_a, 1)
            nc.vector.tensor_tensor(lb_t[:, 4, :], lb_t[:, 2, :], lb_t[:, 3, :], ALU.add).then_inc(softmax_v, 1)
            dve.wait_ge(softmax_a, 2)
            link(nc.vector.reciprocal(lb_t[:, 3, :], lb_t[:, 4, :]))
            link(nc.vector.tensor_tensor(lb_t[:, 0, :], lb_t[:, 0, :], lb_t[:, 5, :], ALU.subtract))
            link(nc.vector.tensor_tensor(lb_t[:, 1, :], lb_t[:, 1, :], lb_t[:, 5, :], ALU.subtract))
            link(nc.vector.tensor_tensor(lb_t[:, 2, :], lb_t[:, 2, :], lb_t[:, 3, :], ALU.mult))
            dve.wait_ge(const_landed, 32)
            nc.vector.tensor_copy(level_mask[:, :, :], mask_in[:, :, :])
            dve.wait_ge(c_ready, 1)

            for n in range(EARLY):
                if n >= 2:
                    dve.wait_ge(ada_reduced, n - 1)
                dve.wait_ge(early_landed[n], 16)
                for k in range(KT):
                    ada_part(n, ada_early[:, n, :, :] if n < EARLY - 2 else ada_raw[:, n % 2, :, :], ada_acc[:, n % 2, :], k)
                if n == EARLY - 3:
                    dve.wait_ge(rms_ready, 1)
                    nc.vector.reciprocal(rstd[:, :], rstd[:, :]).then_inc(vv, 1)
                    chain[0] += 1
            dve.wait_ge(ada_reduced, EARLY)
            nc.vector.tensor_tensor(mod[:, 0:16], bank[0][:, 0:16], adab[:, 0:16], ALU.add).then_inc(mod_ready, 1)

            mods = [1]

            def norm(n):
                final = n == 3 * DEPTH
                g = (3 * n) * KT
                if not final:
                    l, s = n // 3, n % 3
                    dve.wait_ge(mod_ready, mods[0])
                    nw = params[:, ROW_NW + 8 * n:ROW_NW + 8 * n + 8]
                    link(nc.vector.scalar_tensor_tensor(out=scale_a[:, :], in0=mod[:, g + KT:g + 2 * KT], scalar=1.0, in1=nw, op0=ALU.add, op1=ALU.mult))
                    scale = scale_a[:, :]
                else:
                    scale = params[:, ROW_FN:ROW_FN + 8]
                if n == 0:
                    advance(2)
                else:
                    advance(1)
                    dve.wait_ge(rms_ready, n + 1)
                    link(nc.vector.reciprocal(rstd[:, :], rstd[:, :]))

                def low_x(m):
                    dve.wait_ge(x_hi_ready, KT * n + m + 1)
                    nc.vector.scalar_tensor_tensor(out=x_lo[:, m, :], in0=norm_tmp[:, m, :], scalar=mod[:, g + m:g + m + 1], in1=x_hi[:, m, :], op0=ALU.add, op1=ALU.subtract).then_inc(x_lo_ready, 1)
                for m in range(KT):
                    dst = y_t if final else norm_tmp
                    nc.vector.scalar_tensor_tensor(out=dst[:, m, :], in0=h[:, m, :], scalar=scale[:, m:m + 1], in1=rstd[:, :], op0=ALU.mult, op1=ALU.mult).then_inc(y_ready if final else t_ready, 1)
                    if not final and m >= 2:
                        low_x(m - 2)
                if not final:
                    low_x(KT - 2)
                    low_x(KT - 1)
                advance(1 if n else 2)

            def residual(n, factor, tile):
                g = (3 * (n - 1) + 2) * KT
                link(nc.vector.tensor_scalar(coef[:, :], mod[:, g:g + KT], 1.0, factor, ALU.add, ALU.mult))
                for m in range(KT):
                    src = tile(m)
                    nc.vector.scalar_tensor_tensor(out=h[:, m, :], in0=src, scalar=coef[:, m:m + 1], in1=h[:, m, :], op0=ALU.mult, op1=ALU.add).then_inc(h_ready, 1)

            def add_ada(sums, n, count, col=0):
                dve.wait_ge(ada_reduced, n + count)
                nc.vector.tensor_tensor(mod[:, 2 * n:2 * (n + count)], sums[:, col:col + 2 * count], adab[:, 2 * n:2 * (n + count)], ALU.add).then_inc(mod_ready, 1)
                mods[0] += 1

            def ffn(f):
                f0, j0 = ffn_chunk0(f), ffn_job0(f)
                n0, in_w13, ada_steps = ada_plan(f)
                c0 = nxt[0]

                def up(p, parity):
                    dve.wait_ge(gate_free, PAIRS * f + p + 3)
                    dve.wait_ge(chunk_used, f0 + 4 * p + 4)
                    nc.vector.tensor_tensor(gated[:, parity, :], silu_a[:, parity, :], job_bank(j0 + 2 * parity + 1)[:, :], ALU.mult).then_inc(up_free, 1)
                    dve.wait_ge(g_hi_ready, PAIRS * f + p + 1)
                    k = slice(2 * p, 2 * p + 2) if isinstance(p, int) else bass.ds(2 * p, 2)
                    nc.vector.tensor_tensor(g_lo[:, k, :].rearrange("p k t -> p (k t)"), gated[:, parity, :], g_hi[:, k, :].rearrange("p k t -> p (k t)"), ALU.subtract).then_inc(g_lo_ready, 1)

                def ada_step(n, landed, parity, ks):
                    if ks[0] == 0:
                        dve.wait_ge(ada_landed[parity], landed)
                        dve.wait_ge(ada_reduced, n - 1)
                    for k in ks:
                        ada_part(n, ada_raw[:, parity, :, :], ada_acc[:, parity, :], k)

                with dve.Fori(0, PAIRS // 2) as t:
                    for parity in range(2):
                        for i in range(4):
                            if in_w13:
                                ada_step(n0 + 2 * t + parity, landed_count(n0 + parity) + 16 * t, (n0 + parity) % 2, (2 * i, 2 * i + 1))
                            low(None, (c0 + i) % RING, c0 + 4 * parity + i + 1 + 8 * t)
                        up(2 * t + parity, parity)
                nxt[0] += 8 * (PAIRS // 2)
                if in_w13:
                    n = n0 + PAIRS - 1
                    for i in range(4):
                        ada_step(n, landed_count(n), n % 2, (2 * i, 2 * i + 1))
                        advance(1)
                else:
                    advance(4)
                up(PAIRS - 1, 0)
                if in_w13:
                    add_ada(bank[0], n0, PAIRS - 1)
                c0 = nxt[0]
                n1 = n0 + PAIRS if in_w13 else None
                steps = min(DOWN_LOOP, (ALL_CHUNKS - c0) // 4)

                def down_step(t, with_ada):
                    for i in range(4):
                        if with_ada:
                            first = n1 + i // 2
                            ada_step(first + 2 * t, landed_count(first) + 16 * t, first % 2, range(4 * (i % 2), 4 * (i % 2) + 4))
                        low(None, (c0 + i) % RING, c0 + i + 1 + 4 * t)
                if ada_steps:
                    with dve.Fori(0, ada_steps) as t:
                        down_step(t, True)
                if ada_steps < steps:
                    with dve.Fori(ada_steps, steps) as t:
                        down_step(t, False)
                nxt[0] += 4 * steps
                if steps < DOWN_LOOP:
                    advance(2)
                if in_w13:
                    add_ada(job_bank(j0 + 2 * (PAIRS - 2)), n1 - 1, 1 + 2 * ada_steps)
                dve.wait_ge(mod_ready, mods[0])

                def tile(m):
                    if m < KT - 2:
                        dve.wait_ge(down_done, 3 * f + m // 2 + 1)
                    else:
                        dve.wait_ge(chunk_used, f0 + FFN_CHUNKS)
                    return bank[m // 2][:, (m % 2) * T:(m % 2 + 1) * T]
                residual(3 * (f // 2) + 1 + 2 * (f % 2), 0.5, tile)

            def mixer(l):
                c0, j0 = mix_chunk0(l), mix_job0(l)
                m0 = MIX_READS * l
                read = [m0]

                def wait_scored():
                    dve.wait_ge(mix_scored, read[0] + 1)
                    read[0] += 1

                fv = [l]

                dve.wait_ge(ws_landed, 16 * (l + 1))
                dve.wait_ge(const_landed, 32)
                nc.vector.tensor_tensor(ws_raw[:, :, :], ws_raw[:, :, :], tril[:, :].unsqueeze(1).to_broadcast([P, HEADS, P]), ALU.mult).then_inc(ws_masked, 1)
                advance(4)
                for b in range(2):
                    wait_scored()
                    nc.vector.tensor_copy(ws_t[:, 4 * b:4 * b + 4, :].rearrange("p g t -> p (g t)"), bank[b][:, :]).then_inc(mix_read, 1)
                advance(4)

                f0 = 0 if l == 0 else 4
                dl, fl = flat(decay), flat(logf)
                advance(4)
                dve.wait_ge(f_act, f0 + 4)
                nc.vector.scalar_tensor_tensor(out=fl, in0=fl, scalar=0.0, in1=dl, op0=ALU.min, op1=ALU.subtract).then_inc(f_vec, 1)
                fv[0] += 1
                if l > 0:
                    def per_head(row):
                        return lb_t[:, row, :].unsqueeze(2).to_broadcast([P, HEADS, T])
                    dve.wait_ge(f_vec, fv[0])
                    nc.vector.tensor_tensor(logf[:, :, :], logf[:, :, :], per_head(0), ALU.add).then_inc(f_vec, 1)
                    fv[0] += 1
                    advance(1)
                    dve.wait_ge(f_vec, fv[0])
                    nc.vector.tensor_tensor(decay[:, :, :], logf[:, :, :], per_head(1), ALU.subtract).then_inc(f_vec, 1)
                    fv[0] += 1
                    advance(1)
                    nc.vector.tensor_tensor(logf[:, :, :], logf[:, :, :], per_head(1), ALU.max)
                    advance(1)
                    nc.vector.tensor_tensor(key[:, :, :], key[:, :, :], per_head(2), ALU.mult).then_inc(f_vec, 1)
                    fv[0] += 1
                    advance(3)
                    dve.wait_ge(f_act, f0 + 7)
                    dve.wait_ge(f_vec, fv[0])
                    nc.vector.tensor_tensor(logf[:, :, :], logf[:, :, :], decay[:, :, :], ALU.add).then_inc(f_vec, 1)
                    fv[0] += 1
                else:
                    advance(4)

                def suffix(n, m):
                    pre, d = halves(logf, m), halves(decay, m)
                    mid = pre[:, :, 0, m - 1:m].to_broadcast([P, KT * T // (2 * m), m])
                    if n:
                        dve.wait_ge(vv, chain[0])
                    nc.vector.tensor_tensor(d[:, :, 0, :], mid, pre[:, :, 0, :], ALU.subtract).then_inc(suffix_ready, 1)

                def pairs(n, m):
                    pre, d, w = halves(logf, m), halves(decay, m), halves(pair, m)
                    dve.wait_ge(decay_ready, 16 * l + 2 * n + 2)
                    if n:
                        dve.wait_ge(mix_scored, read[0])
                    nc.vector.tensor_tensor(w[:, :, 0, :], halves(key, m)[:, :, 0, :], d[:, :, 0, :], ALU.mult)
                    nc.vector.tensor_tensor(w[:, :, 1, :], halves(query, m)[:, :, 1, :], d[:, :, 1, :], ALU.mult).then_inc(pair_ready, 1)
                    if m < P:
                        mid = pre[:, :, 0, m - 1:m].to_broadcast([P, KT * T // (2 * m), m])
                        chain[0] += 1
                        nc.vector.tensor_tensor(pre[:, :, 1, :], pre[:, :, 1, :], mid, ALU.add).then_inc(vv, 1)

                def merge(n):
                    for b in range(4):
                        wait_scored()
                        s = score[:, 2 * b:2 * b + 2, :].rearrange("p h (n t) -> p (h n) t", n=NT)
                        src = bank[b][:, :].rearrange("p (a t) -> p a t", t=P)
                        mask = level_mask[:, n, :].unsqueeze(1).to_broadcast([P, 4, P])
                        nc.vector.copy_predicated(s, mask, src).then_inc(mix_read, 1)

                dve.wait_ge(f_vec, fv[0])
                suffix(0, 1)
                advance(2 if l else 4)
                for b in range(4):
                    wait_scored()
                    s = score[:, 2 * b:2 * b + 2, :].rearrange("p h (n t) -> p (h n) t", n=NT)
                    src = bank[b][:, :].rearrange("p (a t) -> p a t", t=P)
                    nc.vector.tensor_tensor(s, src, ident[:, :].unsqueeze(1).to_broadcast([P, 4, P]), ALU.mult).then_inc(mix_read, 1)
                pairs(0, 1)
                suffix(1, 2)
                advance(4)
                merge(0)
                pairs(1, 2)
                suffix(2, 4)
                advance(2)
                dve.wait_ge(proj_taken, PROJ_JOBS * l + 12)
                vt = v_gate[:, :, :].rearrange("p k t -> p (k t)").rearrange("p (a c) -> p a c", c=P)
                for a in range(16):
                    last = nc.vector.bn_stats(ln_stats[:, a, :], vt[:, a, :])
                link(last)
                for a in range(16):
                    last = nc.vector.bn_aggr(ln_mv[:, a, :], ln_stats[:, a, :])
                last.then_inc(ln_var, 1)
                advance(2)
                merge(1)
                pairs(2, 4)
                suffix(3, 8)
                advance(4)
                merge(2)
                dve.wait_ge(ln_std, l + 1)
                link(nc.vector.reciprocal(ln_rstd[:, :], ln_rstd[:, :]))
                for a in range(16):
                    last = nc.vector.tensor_scalar(vt[:, a, :], vt[:, a, :], ln_mv[:, a, 0:1], ln_rstd[:, a:a + 1], ALU.subtract, ALU.mult)
                last.then_inc(v_norm, 1)
                advance(4)
                for b in range(4):
                    wait_scored()
                    u = u_gate[:, 2 * b:2 * b + 2, :].rearrange("p k t -> p (k t)")
                    if b == 0:
                        dve.wait_ge(proj_taken, PROJ_JOBS * l + 16)
                    nc.vector.tensor_tensor(u, u, bank[b][:, :], ALU.mult).then_inc(mix_read, 1)
                pairs(3, 8)
                suffix(4, 16)
                advance(4)
                merge(3)
                pairs(4, 16)
                suffix(5, 32)
                advance(2)
                dve.wait_ge(ya_hi_ready, l + 1)
                nc.vector.tensor_tensor(flat(ya_lo), flat(u_gate), flat(ya_hi), ALU.subtract).then_inc(ya_lo_ready, 1)
                advance(2)
                merge(4)
                pairs(5, 32)
                suffix(6, 64)
                advance(4)
                merge(5)
                pairs(6, 64)
                suffix(7, 128)
                advance(4)
                merge(6)
                pairs(7, 128)
                advance(4)
                for b in range(2):
                    wait_scored()
                    nc.vector.tensor_copy(decay[:, 2 * b:2 * b + 2, :].rearrange("p k t -> p (k t)"), bank[b][:, :]).then_inc(mix_read, 1)
                n0, count = ADA_MIX[l]
                for i in range(4):
                    if i < count:
                        ada_block(n0 + i, ada_mix[:, i, :])
                    advance(1)
                dve.wait_ge(o_taken, 4 * (l + 1))
                dve.wait_ge(proj_taken, PROJ_JOBS * l + 24)
                nc.vector.tensor_tensor(flat(o_t), flat(o_t), flat(og), ALU.mult).then_inc(vv, 1)
                chain[0] += 1
                advance(4)
                dve.wait_ge(o_rms, l + 1)
                dve.wait_ge(vv, chain[0])
                nc.vector.tensor_tensor(flat(o_t), flat(o_t), flat(rms_o), ALU.mult).then_inc(yb_full, 1)
                advance(2)

                def gated_job(jj, gate):
                    q = jj % 4
                    dve.wait_ge(chunk_used, c0 + 64 + 2 * jj + 2)
                    g = gate[:, 2 * q:2 * q + 2, :].rearrange("p k t -> p (k t)")
                    nc.vector.tensor_tensor(g, g, job_bank(j0 + PROJ_JOBS + jj)[:, :], ALU.mult).then_inc(branch_taken, 1)
                    return g

                dve.wait_ge(proj_taken, PROJ_JOBS * (l + 1))
                gated_job(0, ga)
                dve.wait_ge(yb_hi_ready, l + 1)
                nc.vector.tensor_tensor(flat(yb_lo), flat(o_t), flat(yb_hi), ALU.subtract).then_inc(yb_lo_ready, 1)
                advance(2)
                gated_job(1, ga)
                for jj in (2, 3):
                    gated_job(jj, ga)
                    advance(2)
                for q in range(4):
                    g = gated_job(4 + q, gb)
                    dve.wait_ge(branch_taken, 8 * l + 5 + q)
                    a = ga[:, 2 * q:2 * q + 2, :].rearrange("p k t -> p (k t)")
                    nc.vector.tensor_tensor(a, a, g, ALU.add).then_inc(m_full, 1)
                    if q < 3:
                        advance(2)
                    dve.wait_ge(m_hi_ready, 4 * l + q + 1)
                    nc.vector.tensor_tensor(ya_lo[:, 2 * q:2 * q + 2, :].rearrange("p k t -> p (k t)"), a, ya_hi[:, 2 * q:2 * q + 2, :].rearrange("p k t -> p (k t)"), ALU.subtract).then_inc(m_lo_ready, 1)
                advance(2)
                n0, count = ADA_MIX[l]
                add_ada(bank[1], n0, count)
                dve.wait_ge(mod_ready, mods[0])

                def tile(m):
                    jj = 8 + m // 2
                    if m % 2 == 0:
                        if m:
                            advance(2)
                        dve.wait_ge(chunk_used, c0 + 64 + 2 * jj + 2)
                    return job_bank(j0 + PROJ_JOBS + jj)[:, (m % 2) * T:(m % 2 + 1) * T]
                residual(3 * l + 2, 1.0, tile)

            for l in range(DEPTH):
                norm(3 * l)
                ffn(2 * l)
                norm(3 * l + 1)
                mixer(l)
                norm(3 * l + 2)
                ffn(2 * l + 1)
            norm(3 * DEPTH)

        @block.tensor
        def _(pe):
            def mm(out_, lhs, rhs, start, stop=False):
                return nc.tensor.matmul(out_, lhs, rhs, start=start, stop=stop, skip_group_check=True)

            def tiles(slot, k, m):
                at = k * JC + m * P
                return w_hi[:, slot, at:at + P], w_lo[:, slot, at:at + P]

            def three(out_, w, xs, start):
                (wh, wl), (xh, xl) = w, xs
                mm(out_, wh, xh, start)
                mm(out_, wh, xl, False)
                return mm(out_, wl, xh, False)

            def job(b, slot0, waits, src, token_major=False, ready=None):
                hi, lo = src
                for q in range(2):
                    slot = (slot0 + q) % RING
                    pe.wait_ge(lo_ready, waits[q])
                    for k in range(KC):
                        kk = KC * q + k
                        if ready is not None:
                            pe.wait_ge(ready[0], ready[1] + kk // ready[2] + 1)
                        for m in range(2):
                            start = kk == 0 and m == 0
                            dst = b[:, m * T:(m + 1) * T]
                            if token_major:
                                at = k * JC
                                whl = w_hi[:, slot, at:at + JC], w_lo[:, slot, at:at + JC]
                                xt = hi[:, kk, m * P:(m + 1) * P], lo[:, kk, m * P:(m + 1) * P]
                                mm(dst, xt[0], whl[0], start)
                                mm(dst, xt[0], whl[1], False)
                                last = mm(dst, xt[1], whl[0], False)
                            else:
                                last = three(dst, tiles(slot, k, m), (hi[:, kk, :], lo[:, kk, :]), start)
                    if q == 0:
                        last.then_inc(chunk_used, 1)
                return last

            def reduce_block(n, acc, dst):
                pe.wait_ge(ada_summed, KT * (n + 1))
                mm(dst[:, 0:1], acc[:, 0:P], ones[:, 0:1], True, True)
                mm(dst[:, 1:2], acc[:, P:2 * P], ones[:, 0:1], True, True).then_inc(ada_reduced, 1)

            def norm_part(n, m):
                pe.wait_ge(sq_ready, KT * n + m + 1)
                last = mm(norm_bank[n][:, 0:T], ones[:, :], norm_tmp[:, m, :], m == 0, m == KT - 1)
                if m == KT - 1:
                    last.then_inc(sum_ready, 1)

            pe.wait_ge(small_landed, 96)
            pe.wait_ge(ones_ready, 1)
            nc.tensor.transpose(bank[1][:, 0:ROWS], rows_in[0:ROWS, 0, :], ident[0:ROWS, 0:ROWS])
            for l in range(DEPTH):
                last = nc.tensor.transpose(bank[1][:, P + 72 * l:P + 72 * (l + 1)], rows_in[0:72, 1 + l, :], ident[0:72, 0:72])
            last.then_inc(rows_turned, 1)
            pe.wait_ge(x_landed, 16)
            for q in range(4):
                for i in range(4):
                    k, n = 2 * q + i // 2, i % 2
                    last = nc.tensor.transpose(bank[4 + q][:, i * P:(i + 1) * P], x_in[:, n, k * P:(k + 1) * P], ident[:, :])
                last.then_inc(x_turned, 1)

            for m in range(KT):
                norm_part(0, m)
            for n in range(EARLY):
                reduce_block(n, ada_acc[:, n % 2, :], bank[0][:, 2 * n:2 * n + 2])

            def ffn(f):
                c0, j0 = ffn_chunk0(f), ffn_job0(f)
                n0, in_w13, ada_steps = ada_plan(f)
                n = 3 * (f // 2) + 2 * (f % 2)
                src = (x_hi, x_lo)

                def reduce_at(n_, parity, b, col):
                    pe.wait_ge(ada_summed, KT * n_ + KT)
                    acc = ada_acc[:, parity, :]
                    for m in range(2):
                        dst = b[:, bass.ds(col + m, 1)] if not isinstance(col, int) else b[:, col + m:col + m + 1]
                        last = mm(dst, acc[:, m * P:(m + 1) * P], ones[:, 0:1], True, True)
                    last.then_inc(ada_reduced, 1)

                def do_pair(p, parity, first=False):
                    for i, free in enumerate((gate_free, up_free)):
                        pe.wait_ge(free, PAIRS * f + p + 1)
                        at = c0 + 4 * p + 2 * i + 1
                        last = job(job_bank(j0 + 2 * parity + i), c0 + 2 * i, (at, at + 1), src,
                                   ready=(x_lo_ready, KT * n, 1) if first and i == 0 else None)
                        last.then_inc(chunk_used, 1)
                        if in_w13 and not first and i == 0:
                            reduce_at(n0 + p - 1, (n0 + parity + 1) % 2, bank[0], 2 * p - 2)

                do_pair(0, 0, True)
                with pe.Fori(0, PAIRS // 2) as t:
                    do_pair(2 * t + 1, 1)
                    do_pair(2 * t + 2, 0)

                if in_w13:
                    pe.wait_ge(mod_ready, mod_count(f))
                d0 = c0 + 4 * PAIRS

                def down_tile(k, slot, m, start):
                    ks = slice(k, k + 1) if isinstance(k, int) else bass.ds(k, 1)
                    hi = g_hi[:, ks, :].rearrange("p k t -> p (k t)")
                    lo = g_lo[:, ks, :].rearrange("p k t -> p (k t)")
                    w = w_hi[:, slot, m * P:(m + 1) * P], w_lo[:, slot, m * P:(m + 1) * P]
                    return three(bank[m // 2][:, (m % 2) * T:(m % 2 + 1) * T], w, (hi, lo), start)

                n1 = n0 + PAIRS if in_w13 else None
                sums = job_bank(j0 + 2 * (PAIRS - 2))
                if in_w13:
                    pe.wait_ge(gate_free, PAIRS * f + PAIRS + 1)

                def down_step(t, with_ada, first=False):
                    for i in range(4):
                        pe.wait_ge(lo_ready, d0 + 4 * t + i + 1)
                        pe.wait_ge(g_lo_ready, PAIRS * f + 2 * t + i // 2 + 1)
                        for m in range(KT):
                            last = down_tile(4 * t + i, (d0 + i) % RING, m, first and i == 0 and m % 2 == 0)
                        last.then_inc(chunk_used, 1)
                        if with_ada and i % 2:
                            reduce_at(n1 - 1 + 2 * t + i // 2, (n1 - 1 + i // 2) % 2, sums, 4 * t + 2 * (i // 2))
                down_step(0, in_w13 > 0, True)
                if ada_steps > 1:
                    with pe.Fori(1, ada_steps) as t:
                        down_step(t, True)
                if max(ada_steps, 1) < DOWN_LOOP:
                    with pe.Fori(max(ada_steps, 1), DOWN_LOOP) as t:
                        down_step(t, False)
                pe.wait_ge(lo_ready, d0 + HT)
                pe.wait_ge(g_lo_ready, PAIRS * (f + 1))
                for m in range(KT):
                    for k in (HT - 2, HT - 1):
                        last = down_tile(k, (d0 + k) % RING, m, False)
                    if m == KT - 1:
                        last.then_inc(chunk_used, 2)
                    elif m % 2:
                        last.then_inc(down_done, 1)
                    if m == 0 and in_w13:
                        c = 2 * ada_steps
                        reduce_at(n1 - 1 + c, (n1 - 1 + c) % 2, sums, 2 * c)
                    if m >= 3:
                        norm_part(n + 1, m - 3)
                for m in range(KT - 3, KT):
                    norm_part(n + 1, m)

            def mod_count(f):
                return {0: 2, 1: 5, 2: 7}[f]

            def mixer(l):
                c0, j0 = mix_chunk0(l), mix_job0(l)
                m0 = MIX_READS * l
                done = [m0]
                src = (x_hi, x_lo)

                def group(g, token_major=False):
                    for j in (2 * g, 2 * g + 1):
                        if j >= 4:
                            pe.wait_ge(proj_taken, PROJ_JOBS * l + j - 3)
                        at = c0 + 2 * j
                        last = job(job_bank(j0 + j), at, (at + 1, at + 2), src, token_major,
                                   ready=(x_lo_ready, KT * (3 * l + 1), 1) if j == 0 else None)
                        last.then_inc(chunk_used, 1)

                def wait_bank():
                    pe.wait_ge(mix_read, done[0] - 3)

                def scored(last):
                    last.then_inc(mix_scored, 1)
                    done[0] += 1

                def score_level(lhs, rhs):
                    for b in range(4):
                        if done[0] >= m0 + 6:
                            wait_bank()
                        for i in range(4):
                            hh, nn = 2 * b + i // 2, i % 2
                            last = mm(bank[b][:, i * P:(i + 1) * P], lhs[:, hh, nn * P:(nn + 1) * P], rhs[:, hh, nn * P:(nn + 1) * P], True, True)
                        scored(last)

                group(0)
                pe.wait_ge(ws_masked, l + 1)
                for b in range(2):
                    for i in range(4):
                        last = nc.tensor.transpose(bank[b][:, i * P:(i + 1) * P], ws_raw[:, 4 * b + i, :], ident[:, :])
                    scored(last)
                for g in (1, 2, 3):
                    group(g)
                group(4, True)
                pe.wait_ge(mix_read, m0 + 2)
                pe.wait_ge(proj_taken, PROJ_JOBS * l + 8)
                pe.wait_ge(f_vec, 1 if l == 0 else 5)
                score_level(key, query)
                for n in range(3):
                    group(5 + n, n == 0)
                    pe.wait_ge(pair_ready, 8 * l + n + 1)
                    score_level(pair, pair)
                group(8, True)
                pe.wait_ge(v_norm, l + 1)
                pe.wait_ge(bias_landed, 16 * (l + 1))
                vt = v_gate[:, :, :].rearrange("p k t -> p (k t)").rearrange("p (n g c) -> p n g c", n=NT, c=P)
                for b in range(4):
                    wait_bank()
                    for i in range(4):
                        g, nn = 2 * b + i // 2, i % 2
                        dst = bank[b][:, i * P:(i + 1) * P]
                        mm(dst, vt[:, nn, g, :], ws_t[:, g, :], True)
                        last = mm(dst, ones[0:1, :], bias_row[0:1, g, :], False, True)
                    scored(last)
                for n in range(3, 7):
                    group(6 + n, n == 3)
                    pe.wait_ge(pair_ready, 8 * l + n + 1)
                    score_level(pair, pair)
                group(13)
                pe.wait_ge(pair_ready, 8 * l + 8)
                for b in range(2):
                    wait_bank()
                    for i in range(4):
                        hh = 4 * b + i
                        last = mm(bank[b][:, i * P:(i + 1) * P], pair[:, hh, 0:P], pair[:, hh, P:2 * P], True, True)
                    scored(last)
                group(14)
                pe.wait_ge(mix_read, m0 + MIX_READS)
                vv_ = val[:, :, :].rearrange("p k t -> p (k t)").rearrange("p (n h c) -> p n h c", n=NT, c=P)
                cross = decay[:, 0:4, :].rearrange("p k (a t) -> p (k a) t", t=P)
                for b in range(4):
                    for i in range(4):
                        hh, nn = 2 * b + i // 2, i % 2
                        dst = bank[b][:, i * P:(i + 1) * P]
                        last = mm(dst, vv_[:, nn, hh, :], score[:, hh, nn * P:(nn + 1) * P], True, nn == 0)
                        if nn == 1:
                            last = mm(dst, vv_[:, 0, hh, :], cross[:, hh, :], False, True)
                    last.then_inc(o_done, 1)
                group(15)
                for b in range(4):
                    pe.wait_ge(o_taken, 4 * l + b + 1)
                    mm(bank[b][:, :], ones[:, :], sq_o[:, 2 * b:2 * b + 2, :].rearrange("p k t -> p (k t)"), True, True).then_inc(o_summed, 1)

                def out_jobs(b, operand, ready, count, tiles_per_count=None):
                    for q in range(4):
                        jj = 4 * b + q
                        if jj < 4:
                            pe.wait_ge(proj_taken, PROJ_JOBS * l + PROJ_JOBS - 3 + jj)
                        else:
                            pe.wait_ge(branch_taken, 8 * l + jj - 3)
                        if q == 0 and not tiles_per_count:
                            pe.wait_ge(ready, count)
                        at = c0 + 64 + 2 * jj
                        job(job_bank(j0 + PROJ_JOBS + jj), at, (at + 1, at + 2), operand,
                            ready=(ready, count, tiles_per_count) if q == 0 and tiles_per_count else None).then_inc(chunk_used, 1)
                        if b == 2 and q:
                            norm_part(3 * l + 2, 2 * q - 2)
                            norm_part(3 * l + 2, 2 * q - 1)
                out_jobs(0, (ya_hi, ya_lo), ya_lo_ready, l + 1)
                out_jobs(1, (yb_hi, yb_lo), yb_lo_ready, l + 1)
                pe.wait_ge(o_rms, l + 1)
                n0, count = ADA_MIX[l]
                for i in range(count):
                    reduce_block(n0 + i, ada_mix[:, i, :], bank[1][:, 2 * i:2 * i + 2])
                out_jobs(2, (ya_hi, ya_lo), m_lo_ready, 4 * l, 2)
                norm_part(3 * l + 2, KT - 2)
                norm_part(3 * l + 2, KT - 1)

            for l in range(DEPTH):
                ffn(2 * l)
                mixer(l)
                ffn(2 * l + 1)
            for n in range(NT):
                for q in range(4):
                    for i in range(2):
                        k = 2 * q + i
                        pe.wait_ge(y_ready, k + 1)
                        last = nc.tensor.transpose(bank[4 * n + q][:, i * P:(i + 1) * P], y_t[:, k, n * P:(n + 1) * P], ident[:, :])
                    last.then_inc(y_turned, 1)


_INS = ['x', 'c', 'w_in', 'gmlp_ws', 'gmlp_b', 'hgrn_lb_logits', 'w_branch_a', 'w_branch_b', 'w_out',
        'ffn_w13', 'ffn_w2', 'norm_w', 'ada_w', 'ada_b', 'final_norm_w']


def _constants():
    i = np.arange(P)
    s, t = i[:, None], i[None, :]
    masks = [(s // (2 * m) == t // (2 * m)) & (s % (2 * m) < m) & (t % (2 * m) >= m) for m in LEVELS]
    return {
        'ident': np.eye(P, dtype=np.float32),
        'level_mask': np.ascontiguousarray(np.stack(masks, 1).astype(np.float32)),
        'tril': np.tril(np.ones((P, P), np.float32)),
    }


def kernel(**inputs):
    import concourse.bacc as _bacc
    from concourse.bass_utils import run_bass_kernel_spmd as _run

    nc = _bacc.Bacc("TRN2", target_bir_lowering=False, num_devices=1)
    arrays = {f"in_{n}": np.ascontiguousarray(inputs[n]) for n in _INS}
    arrays.update({f"const_{n}": a for n, a in _constants().items()})
    args = [nc.dram_tensor(n, a.shape, mybir.dt.from_np(a.dtype), kind="ExternalInput").ap() for n, a in arrays.items()]
    args.append(nc.dram_tensor("y", (1, T, D), F32, kind="ExternalOutput").ap())
    trunk(nc, *args)
    r = _run(nc, [arrays], core_ids=[0])
    return r.results[0]["y"]
```

```python
from contextlib import ExitStack

import numpy as np

import concourse.bass as bass
from concourse import mybir

F32 = mybir.dt.float32
F32R = mybir.dt.float32r
U8 = mybir.dt.uint8
ALU = mybir.AluOpType
ACT = mybir.ActivationFunctionType

P = 128
DEPTH = 2
D = 1024
T = 256
KT = D // P
NT = T // P
HID = 2816
HT = HID // P
EPS = 1e-6
HEADS = 8
N_ADA = 9

RING = 4
CHUNK = 1024
SQ_V = 4
WARM = (4, 9, 16, 12)
WARM_START = 2
KC = 4
JC = 256
PAIRS = HID // JC
ADA_BLOCKS = N_ADA * D // 256

FFN_CHUNKS = 4 * PAIRS + HT
GROUPS = 16
MIX_CHUNKS = 4 * GROUPS + 3 * 8
LAYER_CHUNKS = 2 * FFN_CHUNKS + MIX_CHUNKS
ALL_CHUNKS = DEPTH * LAYER_CHUNKS
FFN_JOBS = 2 * PAIRS
PROJ_JOBS = 2 * GROUPS
MIX_JOBS = PROJ_JOBS + 12
LAYER_JOBS = 2 * FFN_JOBS + MIX_JOBS

LEVELS = (1, 2, 4, 8, 16, 32, 64)
HALF = P // 2
MIX_YA = 2 + 4 + 3 * 2 + 4
MIX_READS = 2 + 4 + 2 * len(LEVELS) + 4 + 2
DOWN_LOOP = (HT - 2) // 4
LATE = DOWN_LOOP
MIX_BLOCKS = 8
ADA_PLAN = {0: 8, 1: 32, 2: 48}
ADA_MIX = {0: 24, 1: 64}
EARLY = 8
EARLY_V = 4

ROW_C, ROW_LB, ROW_NW, ROW_FN, ROWS = 0, 8, 24, 72, 80


def trunk(nc, x, c, w_in, gmlp_ws, gmlp_b, lb_logits, w_a, w_b, w_o, w13, w2, norm_w, ada_w, ada_b,
          final_w, ident_in, level_mask_in, tril_in, out):
    ctx = ExitStack()
    with ctx:
        def sb(name, shape, dt=F32, stack=ctx):
            return stack.enter_context(nc.sbuf_tensor(name, shape, dt))

        def sem(name):
            return ctx.enter_context(nc.semaphore(name))

        raw = sb("raw", [P, RING, CHUNK])
        w_hi = sb("w_hi", [P, RING, CHUNK], F32R)
        w_lo = sb("w_lo", [P, RING, CHUNK], F32R)
        ada_raw = sb("ada_raw", [P, 2, KT, 256])
        ada_acc = sb("ada_acc", [P, 2, 256])
        h = sb("h", [P, KT, T])
        x_hi = sb("x_hi", [P, KT, T], F32R)
        x_lo = sb("x_lo", [P, KT, T], F32R)
        mod = sb("mod", [P, DEPTH * N_ADA * KT])
        params = sb("params", [P, ROWS])
        adab = sb("adab", [P, DEPTH * N_ADA * KT])
        c_act = sb("c_act", [P, KT])
        scale_a = sb("scale_a", [P, KT])
        coef = sb("coef", [P, KT])
        rstd = sb("rstd", [P, T])
        ones = sb("ones", [P, P])
        act_scratch = sb("act_scratch", [P, 1])
        eps_t = sb("eps_t", [P, 2])
        ident = sb("ident", [P, P])
        tril = sb("tril", [P, P])
        level_mask = sb("level_mask", [P, len(LEVELS), HALF], U8)
        lb_t = sb("lb_t", [P, 6, HEADS])
        mix_bias = sb("mix_bias", [P, HEADS, P])
        ln_stats = sb("ln_stats", [P, 16, 6])
        ln_mv = sb("ln_mv", [P, 16, 2])
        ln_rstd = sb("ln_rstd", [P, 16])
        ws_t = sb("ws_t", [P, HEADS, P])

        with ExitStack() as tmp:
            silu_a = sb("silu_a", [P, 2, 512], F32, tmp)
            gated = sb("gated", [P, 2, 512], F32, tmp)
        with ExitStack() as tmp:
            ada_mix = sb("ada_mix", [P, MIX_BLOCKS, 256], F32, tmp)
        norm_tmp = sb("norm_tmp", [P, KT, T])

        with ExitStack() as tmp:
            g_hi = sb("g_hi", [P, HT, T], F32R, tmp)
            g_lo = sb("g_lo", [P, HT, T], F32R, tmp)
        def unit(name, dt=F32, stack=ctx):
            return sb(name, [P, KT, T], dt, stack)
        with ExitStack() as tmp:
            rows_in = sb("rows_in", [P, 3, P], F32, tmp)
            x_in = sb("x_in", [P, NT, D], F32, tmp)
            mask_in = sb("mask_in", [P, len(LEVELS), HALF], F32, tmp)
            y_out = sb("y_out", [P, NT, D], F32, tmp)
            y_t = sb("y_t", [P, KT, T], F32, tmp)
            ada_early = sb("ada_early", [P, EARLY - 2, KT, 256], F32, tmp)
            early_acc = sb("early_acc", [P, EARLY_V, 256], F32, tmp)
            early_row = sb("early_row", [1, EARLY - EARLY_V, 256], F32, tmp)
        with ExitStack() as tmp:
            yb_hi = unit("yb_hi", F32R, tmp)
            yb_lo = unit("yb_lo", F32R, tmp)
        key = unit("key")
        query = unit("query")
        logf = unit("logf")
        pair = unit("pair")
        decay = unit("decay")
        score = unit("score")
        val = unit("val")
        with ExitStack() as tmp:
            v_gate = unit("v_gate", F32, tmp)
        ya_hi = unit("ya_hi", F32R)
        u_gate = unit("u_gate")
        ya_lo = unit("ya_lo", F32R)
        with ExitStack() as tmp:
            ada_late = sb("ada_late", [P, LATE, 256], F32, tmp)
        ga = unit("ga")
        ws_raw = sb("ws_raw", [P, HEADS, P])
        o_t, gb, og = logf, pair, u_gate
        sq_o, rms_o = key, query

        bank = [ctx.enter_context(nc.psum_tensor(f"bank{i}", [P, 512], F32)) for i in range(8)]

        raw_landed = [sem(f"raw_landed{i}") for i in range(RING)]
        hi_ready, lo_ready, chunk_used = (sem(n) for n in ("hi_ready", "lo_ready", "chunk_used"))
        gate_free, up_free = sem("gate_free"), sem("up_free")
        g_hi_ready, g_lo_ready = sem("g_hi_ready"), sem("g_lo_ready")
        proj_taken, branch_taken = sem("proj_taken"), sem("branch_taken")
        small_landed, x_landed, const_landed = sem("small_landed"), sem("x_landed"), sem("const_landed")
        ws_landed, bias_landed = sem("ws_landed"), sem("bias_landed")
        ones_ready, consts_ready = sem("ones_ready"), sem("consts_ready")
        rows_turned, params_ready, c_ready = sem("rows_turned"), sem("params_ready"), sem("c_ready")
        x_turned = sem("x_turned")
        early_landed = [sem(f"early_landed{i}") for i in range(EARLY)]
        ada_landed = [sem("ada_landed0"), sem("ada_landed1")]
        row_summed, row_copied = sem("row_summed"), sem("row_copied")
        down_done, sq_summed = sem("down_done"), sem("sq_summed")
        ada_summed, ada_reduced, mod_ready = sem("ada_summed"), sem("ada_reduced"), sem("mod_ready")
        h_ready, sq_ready, sum_ready, rms_ready = sem("h_ready"), sem("sq_ready"), sem("sum_ready"), sem("rms_ready")
        t_ready, x_hi_ready, x_lo_ready, vv = sem("t_ready"), sem("x_hi_ready"), sem("x_lo_ready"), sem("vv")
        aa = sem("aa")
        softmax_v, softmax_a = sem("softmax_v"), sem("softmax_a")
        ws_masked, mix_scored, mix_read = sem("ws_masked"), sem("mix_scored"), sem("mix_read")
        f_act, f_vec = sem("f_act"), sem("f_vec")
        suffix_ready, decay_ready, pair_ready = sem("suffix_ready"), sem("decay_ready"), sem("pair_ready")
        ln_var, ln_std, v_norm = sem("ln_var"), sem("ln_std"), sem("v_norm")
        ya_hi_ready, ya_lo_ready = sem("ya_hi_ready"), sem("ya_lo_ready")
        o_done, o_taken, o_summed, o_rms = sem("o_done"), sem("o_taken"), sem("o_summed"), sem("o_rms")
        yb_full, yb_hi_ready, yb_lo_ready = sem("yb_full"), sem("yb_hi_ready"), sem("yb_lo_ready")
        m_full, m_hi_ready, m_lo_ready = sem("m_full"), sem("m_hi_ready"), sem("m_lo_ready")
        y_ready, y_turned, y_copied, y_stored = sem("y_ready"), sem("y_turned"), sem("y_copied"), sem("y_stored")

        def ffn_chunk0(f):
            return (f // 2) * LAYER_CHUNKS + (f % 2) * (FFN_CHUNKS + MIX_CHUNKS)

        def ffn_job0(f):
            return (f // 2) * LAYER_JOBS + (f % 2) * (FFN_JOBS + MIX_JOBS)

        def mix_chunk0(l):
            return l * LAYER_CHUNKS + FFN_CHUNKS

        def mix_job0(l):
            return l * LAYER_JOBS + FFN_JOBS

        def job_bank(j):
            return bank[4 + j % 4]

        norm_bank = {0: bank[2], 1: bank[7], 2: bank[0], 3: bank[7], 4: bank[7], 5: bank[0], 6: bank[7]}

        def landed_count(n):
            return 16 * (n // 2 - EARLY // 2 + 1)

        def early(n):
            return ada_early[:, n, :, :] if n < EARLY - 2 else ada_raw[:, n % 2, :, :]

        def row_bank(i):
            return bank[1 + 2 * (i % 2)]

        def has_ada(f):
            return f in ADA_PLAN

        def halves(t, m):
            flat = t[:, :, :].rearrange("p h t -> p (h t)")
            return flat.rearrange("p (b two m) -> p b two m", two=2, m=m)

        block = ctx.enter_context(nc.Block())

        w13_v = w13.rearrange("l w (q k p) c -> l w q p k c", k=KC, p=P)
        w2_v = w2.rearrange("l w (k p) c -> l w p k c", p=P)
        ada_v = ada_w.rearrange("l (k p) c -> l p k c", p=P)
        in_v = w_in.rearrange("l (q k p) c -> l q p k c", k=KC, p=P)
        mix_v = [w.rearrange("l (q k p) c -> l q p k c", k=KC, p=P) for w in (w_a, w_b, w_o)]

        @block.sync
        def _(sp):
            def load(slot, src, wait):
                if wait is not None:
                    sp.wait_ge(lo_ready, wait)
                dst = raw[:, slot, :]
                if len(src.shape) == 3:
                    dst = dst.rearrange("p (k c) -> p k c", k=KC)
                sp.dma_start(dst, src).then_inc(raw_landed[slot], 16)

            def ffn(f):
                l, w, c0 = f // 2, f % 2, ffn_chunk0(f)

                def pair_loads(p, first=False):
                    for i in range(4):
                        q, up = (i // 2, i % 2) if first else (i % 2, i // 2)
                        col = p * JC + up * HID
                        load((c0 + i) % RING, w13_v[l, w, q][:, :, bass.ds(col, JC)],
                             None if first and f == 0 else c0 + 4 * p + i - RING + 1)
                pair_loads(0, True)
                if f == 0:
                    sp.dma_start(tril[:, :], tril_in).then_inc(const_landed, 16)
                    sp.dma_start(mask_in[:, :, :], level_mask_in).then_inc(const_landed, 16)
                with sp.Fori(1, PAIRS) as p:
                    pair_loads(p)
                d0 = c0 + 4 * PAIRS
                with sp.Fori(0, HT // 4) as t:
                    for i in range(4):
                        load((d0 + i) % RING, w2_v[l, w][:, bass.ds(4 * t + i, 1), :].rearrange("p k c -> p (k c)"),
                             d0 + 4 * t + i - RING + 1)
                for k in range(HT // 4 * 4, HT):
                    load((d0 + k) % RING, w2_v[l, w][:, k, :], d0 + k - RING + 1)

            def mixer(l):
                c0 = mix_chunk0(l)
                def segment(s, half, start=0):
                    first = s * D + 4 * D if half else s * -D + 3 * D
                    for i in range(start, 8):
                        at = c0 + 32 * half + i
                        load(at % RING, in_v[l, i % 2][:, :, bass.ds(first + (i // 2) * JC, JC)], at + 8 * s - RING + 1)

                for i in range(4):
                    load((c0 + i) % RING, in_v[l, i // 2][:, :, 3 * D + (i % 2) * JC:3 * D + (i % 2 + 1) * JC], c0 + i - RING + 1)
                segment(0, 0, 4)
                with sp.Fori(1, 4) as s:
                    segment(s, 0)
                with sp.Fori(0, 4) as s:
                    segment(s, 1)
                for b in range(3):
                    for i in range(8):
                        at = c0 + 64 + 8 * b + i
                        load(at % RING, mix_v[b][l, i % 2][:, :, (i // 2) * JC:(i // 2 + 1) * JC], at - RING + 1)

            for i in range(EARLY):
                n = i // 2 + i % 2 * EARLY_V
                if i == 1:
                    sp.wait_ge(small_landed, 96)
                sp.dma_start(early(n), ada_v[0][:, :, n * 256:(n + 1) * 256]).then_inc(early_landed[n], 16)
                if i == 1:
                    sp.dma_start(x_in[:, :, :], x[0].rearrange("(n p) d -> p n d", p=P)).then_inc(x_landed, 16)
            for l in range(DEPTH):
                ffn(2 * l)
                mixer(l)
                ffn(2 * l + 1)
            for n in range(NT):
                sp.wait_ge(y_copied, 4 * (n + 1))
                sp.dma_start(out[0, n * P:(n + 1) * P, :], y_out[:, n, :]).then_inc(y_stored, 16)
            sp.wait_ge(y_stored, 16 * NT)

        @block.gpsimd
        def _(pool):
            def ada_load(n, blk, parity):
                pool.wait_ge(ada_summed, KT * n - KT)
                l, b = blk
                pool.dma_start(ada_raw[:, parity, :, :], ada_v[l][:, :, bass.ds(b * 256, 256)]).then_inc(ada_landed[parity], 16)

            def ws_load(l):
                if l:
                    pool.wait_ge(mix_read, MIX_READS * l)
                    pool.wait_ge(mix_scored, MIX_READS * l)
                pool.dma_start(ws_raw[:, :, :], gmlp_ws[l].rearrange("g t s -> t g s")).then_inc(ws_landed, 16)
                pool.dma_start(mix_bias[:, :, :], gmlp_b[l].partition_broadcast(P)).then_inc(bias_landed, 16)

            def run(n0, count):
                l, b0 = n0 // ADA_BLOCKS, n0 % ADA_BLOCKS
                with pool.Fori(0, count // 2) as t:
                    for i in range(2):
                        ada_load(n0 + 2 * t + i, (l, b0 + 2 * t + i), (n0 + i) % 2)
                if count % 2:
                    ada_load(n0 + count - 1, (l, b0 + count - 1), (n0 + count - 1) % 2)

            pool.wait_ge(ada_summed, KT * EARLY)
            ws_load(0)
            run(EARLY, ADA_BLOCKS - EARLY)
            last = ADA_PLAN[2]
            run(ADA_BLOCKS, last - ADA_BLOCKS)
            ws_load(1)
            run(last, 2 * ADA_BLOCKS - last)

        @block.scalar
        def _(act):
            nxt = [0]

            def split(chunk, slot, wait_slot=True):
                act.wait_ge(raw_landed[slot], 16 * (chunk // RING + 1))
                if wait_slot:
                    act.wait_ge(chunk_used, chunk - RING + 1)
                nc.scalar.activation(w_hi[:, slot, :], raw[:, slot, :], ACT.Copy).then_inc(hi_ready, 1)

            def split_at(base, step, i):
                c = base + i
                slot = c % RING
                act.wait_ge(raw_landed[slot], 16 * (c // RING + 1) + 16 * step)
                act.wait_ge(chunk_used, c - RING + 1 + RING * step)
                nc.scalar.activation(w_hi[:, slot, :], raw[:, slot, :], ACT.Copy).then_inc(hi_ready, 1)

            def advance(n):
                for _ in range(n):
                    if nxt[0] < ALL_CHUNKS:
                        split(nxt[0], nxt[0] % RING, nxt[0] >= RING)
                        nxt[0] += 1

            act.dma_start(rows_in[ROW_C:ROW_C + 8, 0, :], c.rearrange("o (k p) -> (o k) p", p=P)).then_inc(small_landed, 16)
            act.dma_start(rows_in[ROW_LB:ROW_NW, 0, :], lb_logits.rearrange("l (k p) -> (l k) p", p=P)).then_inc(small_landed, 16)
            act.dma_start(rows_in[ROW_NW:ROW_FN, 0, :], norm_w.rearrange("l s (k p) -> (l s k) p", p=P)).then_inc(small_landed, 16)
            act.dma_start(rows_in[ROW_FN:ROWS, 0, :], final_w.rearrange("(k p) -> k p", p=P)).then_inc(small_landed, 16)
            act.dma_start(rows_in[0:72, 1:3, :], ada_b.rearrange("l (k p) -> k l p", p=P)).then_inc(small_landed, 16)
            act.dma_start(ident[:, :], ident_in).then_inc(small_landed, 16)
            act.sem_inc(gate_free, 2)

            act.wait_ge(params_ready, 2)
            nc.scalar.activation(c_act[:, :], params[:, ROW_C:ROW_C + KT], ACT.Silu).then_inc(c_ready, 1)
            act.wait_ge(softmax_v, 1)
            nc.scalar.activation(lb_t[:, 2:4, :], lb_t[:, 0:2, :], ACT.Exp).then_inc(softmax_a, 1)
            act.wait_ge(softmax_v, 2)
            nc.scalar.activation(lb_t[:, 5, :], lb_t[:, 4, :], ACT.Ln).then_inc(softmax_a, 1)
            for q in range(4):
                act.wait_ge(x_turned, q + 1)
                nc.scalar.activation(h[:, 2 * q:2 * q + 2, :].rearrange("p k t -> p (k t)"), bank[4 + q][:, :], ACT.Copy).then_inc(h_ready, 2)

            def copy_row(i):
                act.wait_ge(row_summed, i + 1)
                nc.scalar.activation(early_row[0:1, i, :], row_bank(i)[0:1, 0:256], ACT.Copy).then_inc(row_copied, 1)

            def norm(n):
                nc.scalar.activation(act_scratch[:, :], eps_t[:, 0:1], ACT.Sqrt)
                for m in range(KT):
                    if n % 3 == 2 and m and m % 2 == 0:
                        advance(2)
                    act.wait_ge(h_ready, KT * n + m + 1)
                    nc.scalar.activation(norm_tmp[:, m, :], h[:, m, :], ACT.Square).then_inc(sq_ready, 1)
                if n:
                    advance(1)
                else:
                    copy_row(0)
                act.wait_ge(sum_ready, n + 1)
                nc.scalar.activation(rstd[:, :], norm_bank[n][:, 0:T], ACT.Sqrt, bias=eps_t[:, 0:1], scale=1.0 / D).then_inc(rms_ready, 1)
                if n == 3 * DEPTH:
                    return
                if n == 0:
                    copy_row(1)
                    copy_row(2)
                    advance(2)
                    copy_row(3)
                advance(1)
                shift = (3 * n) * KT
                for m in range(KT):
                    act.wait_ge(t_ready, KT * n + m + 1)
                    nc.scalar.activation(x_hi[:, m, :], norm_tmp[:, m, :], ACT.Identity, bias=mod[:, shift + m:shift + m + 1]).then_inc(x_hi_ready, 1)
                    if n == 0 and m == KT // 2:
                        advance(1)

            def ffn(f):
                c0, j0 = ffn_chunk0(f), ffn_job0(f)
                n_split = nxt[0]

                def gate(p, parity, first=False):
                    act.wait_ge(chunk_used, c0 + 4 if first else c0 + 4 * p + 2)
                    act.wait_ge(up_free, PAIRS * f + p + 1)
                    nc.scalar.activation(silu_a[:, parity, :], job_bank(j0 + 2 * parity)[:, :], ACT.Silu).then_inc(gate_free, 1)
                    act.wait_ge(up_free, PAIRS * f + p + 3)
                    dst = g_hi[:, bass.ds(2 * p, 2), :] if not isinstance(p, int) else g_hi[:, 2 * p:2 * p + 2, :]
                    nc.scalar.activation(dst.rearrange("p k t -> p (k t)"), gated[:, parity, :], ACT.Copy).then_inc(g_hi_ready, 1)

                advance(4)
                gate(0, 0, True)
                with act.Fori(0, PAIRS // 2) as t:
                    for p in (1, 2):
                        for i in range(4):
                            split_at(n_split + 4 * p, 2 * t, i)
                        gate(2 * t + p, p % 2)
                nxt[0] += 8 * (PAIRS // 2)
                n_split = nxt[0]
                steps = min(DOWN_LOOP, (ALL_CHUNKS - n_split) // 4)
                with act.Fori(0, steps) as t:
                    for i in range(4):
                        split_at(n_split, t, i)
                nxt[0] += 4 * steps
                if steps < DOWN_LOOP:
                    advance(2)

            def mixer(l):
                c0, j0 = mix_chunk0(l), mix_job0(l)

                def take(g, fn, dst, token_major=False, **kw):
                    for j in (2 * g, 2 * g + 1):
                        act.wait_ge(chunk_used, c0 + 2 * max(j, 1) + 2)
                        src, q = job_bank(j0 + j), j % 4
                        if token_major:
                            d = dst[:, :, :].rearrange("p k t -> p (k t)").rearrange("p (n d) -> p n d", n=NT)[:, :, q * JC:(q + 1) * JC]
                            s = src[:, :].rearrange("p (n d) -> p n d", n=NT)
                        else:
                            d = dst[:, 2 * q:2 * q + 2, :].rearrange("p k t -> p (k t)")
                            s = src[:, :]
                        nc.scalar.activation(d, s, fn, **kw).then_inc(proj_taken, 1)

                def level(n, m):
                    act.wait_ge(suffix_ready, 8 * l + n + 1)
                    d, pre = halves(decay, m), halves(logf, m)
                    nc.scalar.activation(d[:, :, 0, :], d[:, :, 0, :], ACT.Exp).then_inc(decay_ready, 1)
                    nc.scalar.activation(d[:, :, 1, :], pre[:, :, 1, :], ACT.Exp).then_inc(decay_ready, 1)

                fa = [4 * l]
                fv = [l]

                def f_step(out_, in_, fn, wait_self=True, **kw):
                    if wait_self:
                        act.wait_ge(f_act, fa[0])
                    nc.scalar.activation(out_, in_, fn, **kw).then_inc(f_act, 1)
                    fa[0] += 1

                fl = logf[:, :, :].rearrange("p k t -> p (k t)")
                dl = decay[:, :, :].rearrange("p k t -> p (k t)")
                advance(4)
                take(0, ACT.Copy, logf)
                advance(4)
                take(1, ACT.Copy, logf)
                act.wait_ge(proj_taken, PROJ_JOBS * l + 4)
                f_step(key[:, :, :].rearrange("p k t -> p (k t)"), fl, ACT.Sigmoid, False, scale=-1.0)
                advance(1)
                f_step(dl, fl, ACT.Abs, False)
                advance(1)
                f_step(dl, dl, ACT.Exp, scale=-1.0)
                advance(2)
                f_step(dl, dl, ACT.Ln, bias=eps_t[:, 1:2])
                advance(1)
                take(2, ACT.Silu, query)
                advance(2 if l else 1)
                if l > 0:
                    act.wait_ge(f_vec, fv[0] + 3)
                    f_step(dl, dl, ACT.Abs, False)
                    advance(1)
                    take(3, ACT.Silu, query)
                    f_step(dl, dl, ACT.Exp, scale=-1.0)
                    advance(2)
                    f_step(dl, dl, ACT.Ln, bias=eps_t[:, 1:2])
                    advance(2)
                    level(0, 1)
                    take(4, ACT.Gelu_apprx_tanh, v_gate, True)
                else:
                    advance(2)
                    take(3, ACT.Silu, query)

                def step(g, n, *taken, **kw):
                    advance(2)
                    if n is not None:
                        level(n, 2 ** n)
                    advance(2)
                    if taken:
                        take(g, *taken, **kw)
                if l == 0:
                    step(4, 0, ACT.Gelu_apprx_tanh, v_gate, token_major=True)
                step(5, 1, ACT.Gelu_apprx_tanh, v_gate, token_major=True)
                step(6, 2, ACT.Gelu_apprx_tanh, u_gate)
                step(7, None, ACT.Gelu_apprx_tanh, u_gate)
                act.wait_ge(ln_var, l + 1)
                nc.scalar.activation(ln_rstd[:, :], ln_mv[:, :, 1], ACT.Sqrt, bias=eps_t[:, 0:1]).then_inc(ln_std, 1)
                step(8, 3, ACT.Copy, val, token_major=True)
                step(9, 4)
                act.wait_ge(mix_read, MIX_READS * l + MIX_YA)
                nc.scalar.activation(ya_hi[:, :, :].rearrange("p k t -> p (k t)"), u_gate[:, :, :].rearrange("p k t -> p (k t)"), ACT.Copy).then_inc(ya_hi_ready, 1)
                take(9, ACT.Copy, val, True)
                step(10, 5)
                act.wait_ge(ya_lo_ready, l + 1)
                take(10, ACT.Sigmoid, og)
                step(11, 6, ACT.Sigmoid, og)
                step(12, 7, ACT.Sigmoid, ga)
                step(13, None, ACT.Sigmoid, ga)
                step(14, None, ACT.Sigmoid, gb)
                for b in range(4):
                    act.wait_ge(o_done, 4 * l + b + 1)
                    nc.scalar.activation(o_t[:, 2 * b:2 * b + 2, :].rearrange("p k t -> p (k t)"), bank[b][:, :], ACT.Copy)
                    nc.scalar.activation(sq_o[:, 2 * b:2 * b + 2, :].rearrange("p k t -> p (k t)"), bank[b][:, :], ACT.Square).then_inc(o_taken, 1)
                step(15, None, ACT.Sigmoid, gb)
                for b in range(4):
                    act.wait_ge(o_summed, 4 * l + b + 1)
                    r = rms_o[:, 2 * b:2 * b + 2, :].rearrange("p k t -> p (k t)")
                    nc.scalar.activation(r, bank[b][:, :], ACT.Ln, bias=eps_t[:, 0:1], scale=1.0 / P).then_inc(aa, 1)
                act.wait_ge(aa, 4 * (l + 1))
                rl = rms_o[:, :, :].rearrange("p k t -> p (k t)")
                nc.scalar.activation(rl, rl, ACT.Exp, scale=-0.5).then_inc(o_rms, 1)
                advance(2)
                act.wait_ge(yb_full, l + 1)
                nc.scalar.activation(yb_hi[:, :, :].rearrange("p k t -> p (k t)"), o_t[:, :, :].rearrange("p k t -> p (k t)"), ACT.Copy).then_inc(yb_hi_ready, 1)
                advance(6)
                for b in range(4):
                    if b < 3:
                        advance(2)
                    act.wait_ge(m_full, 4 * l + b + 1)
                    nc.scalar.activation(ya_hi[:, 2 * b:2 * b + 2, :].rearrange("p k t -> p (k t)"), ga[:, 2 * b:2 * b + 2, :].rearrange("p k t -> p (k t)"), ACT.Copy).then_inc(m_hi_ready, 1)
                advance(2)

            for l in range(DEPTH):
                norm(3 * l)
                ffn(2 * l)
                norm(3 * l + 1)
                mixer(l)
                norm(3 * l + 2)
                ffn(2 * l + 1)
            norm(3 * DEPTH)
            for q in range(8):
                act.wait_ge(y_turned, q + 1)
                nc.scalar.activation(y_out[:, q // 4, (q % 4) * 256:(q % 4 + 1) * 256], bank[q][:, 0:256], ACT.Copy).then_inc(y_copied, 1)

        @block.vector
        def _(dve):
            nxt = [0]

            def low(c, slot, value):
                dve.wait_ge(hi_ready, value)
                nc.vector.tensor_tensor(w_lo[:, slot, :], raw[:, slot, :], w_hi[:, slot, :], ALU.subtract).then_inc(lo_ready, 1)

            def advance(n):
                for _ in range(n):
                    if nxt[0] < ALL_CHUNKS:
                        low(nxt[0], nxt[0] % RING, nxt[0] + 1)
                        nxt[0] += 1

            def flat(t):
                return t[:, :, :].rearrange("p k t -> p (k t)")

            chain = [0]

            def link(ins):
                chain[0] += 1
                ins.then_inc(vv, 1)
                dve.wait_ge(vv, chain[0])

            def ada_part(n, block_in, acc, k):
                wk = block_in[:, k, :]
                if k == 0:
                    last = nc.vector.tensor_scalar(acc, wk, c_act[:, 0:1], None, ALU.mult)
                else:
                    dve.wait_ge(ada_summed, KT * n + k)
                    last = nc.vector.scalar_tensor_tensor(out=acc, in0=wk, scalar=c_act[:, k:k + 1], in1=acc, op0=ALU.mult, op1=ALU.add)
                last.then_inc(ada_summed, 1)

            def ada_block(n, acc, between=0):
                dve.wait_ge(ada_landed[n % 2], landed_count(n))
                for k in range(KT):
                    if k == KT // 2:
                        advance(between)
                    ada_part(n, ada_raw[:, n % 2, :, :], acc, k)

            def add_square(n, m):
                dve.wait_ge(sq_ready, KT * n + m + 1)
                if m > 1:
                    dve.wait_ge(vv, chain[0])
                last = nc.vector.tensor_tensor(norm_tmp[:, 0, :], norm_tmp[:, 0, :], norm_tmp[:, m, :], ALU.add)
                if m < SQ_V - 1:
                    last.then_inc(vv, 1)
                    chain[0] += 1
                else:
                    last.then_inc(sq_summed, 1)

            nc.vector.memset(ones[:, :], 1.0).then_inc(ones_ready, 1)
            nc.vector.memset(eps_t[:, 0:1], EPS).then_inc(consts_ready, 1)
            nc.vector.memset(eps_t[:, 1:2], 1.0).then_inc(consts_ready, 1)
            dve.sem_inc(up_free, 2)
            dve.wait_ge(rows_turned, 1)
            nc.vector.tensor_copy(params[:, :], bank[1][:, 0:ROWS]).then_inc(params_ready, 1)
            nc.vector.tensor_copy(adab[:, :], bank[1][:, 128:128 + 144]).then_inc(params_ready, 1)
            dve.wait_ge(params_ready, 2)
            l0, l1 = params[:, ROW_LB:ROW_LB + 8], params[:, ROW_LB + 8:ROW_LB + 16]
            link(nc.vector.tensor_tensor(lb_t[:, 4, :], l0, l1, ALU.max))
            link(nc.vector.tensor_tensor(lb_t[:, 0, :], l0, lb_t[:, 4, :], ALU.subtract))
            nc.vector.tensor_tensor(lb_t[:, 1, :], l1, lb_t[:, 4, :], ALU.subtract).then_inc(softmax_v, 1)
            dve.wait_ge(softmax_a, 1)
            nc.vector.tensor_tensor(lb_t[:, 4, :], lb_t[:, 2, :], lb_t[:, 3, :], ALU.add).then_inc(softmax_v, 1)
            dve.wait_ge(softmax_a, 2)
            link(nc.vector.reciprocal(lb_t[:, 3, :], lb_t[:, 4, :]))
            link(nc.vector.tensor_tensor(lb_t[:, 0, :], lb_t[:, 0, :], lb_t[:, 5, :], ALU.subtract))
            link(nc.vector.tensor_tensor(lb_t[:, 1, :], lb_t[:, 1, :], lb_t[:, 5, :], ALU.subtract))
            link(nc.vector.tensor_tensor(lb_t[:, 2, :], lb_t[:, 2, :], lb_t[:, 3, :], ALU.mult))
            dve.wait_ge(c_ready, 1)

            for n in range(EARLY_V):
                dve.wait_ge(early_landed[n], 16)
                for k in range(KT):
                    ada_part(n, early(n), early_acc[:, n, :], k)
                if n == 1:
                    for m in range(1, SQ_V):
                        add_square(0, m)
                if n == 2:
                    dve.wait_ge(rms_ready, 1)
                    nc.vector.reciprocal(rstd[:, :], rstd[:, :]).then_inc(vv, 1)
                    chain[0] += 1
            advance(3)
            dve.wait_ge(ada_reduced, EARLY)
            dve.sem_inc(ada_summed, KT * (EARLY - EARLY_V))
            nc.vector.tensor_tensor(mod[:, 0:16], bank[0][:, 0:16], adab[:, 0:16], ALU.add).then_inc(mod_ready, 1)

            mods = [1]

            def norm(n):
                final = n == 3 * DEPTH
                g = (3 * n) * KT
                if not final:
                    l, s = n // 3, n % 3
                    dve.wait_ge(mod_ready, mods[0])
                    nw = params[:, ROW_NW + 8 * n:ROW_NW + 8 * n + 8]
                    link(nc.vector.scalar_tensor_tensor(out=scale_a[:, :], in0=mod[:, g + KT:g + 2 * KT], scalar=1.0, in1=nw, op0=ALU.add, op1=ALU.mult))
                    scale = scale_a[:, :]
                else:
                    scale = params[:, ROW_FN:ROW_FN + 8]
                if n:
                    dve.wait_ge(rms_ready, n + 1)
                    link(nc.vector.reciprocal(rstd[:, :], rstd[:, :]))

                def low_x(m):
                    dve.wait_ge(x_hi_ready, KT * n + m + 1)
                    nc.vector.scalar_tensor_tensor(out=x_lo[:, m, :], in0=norm_tmp[:, m, :], scalar=mod[:, g + m:g + m + 1], in1=x_hi[:, m, :], op0=ALU.add, op1=ALU.subtract).then_inc(x_lo_ready, 1)
                for m in range(KT):
                    dst = y_t if final else norm_tmp
                    nc.vector.scalar_tensor_tensor(out=dst[:, m, :], in0=h[:, m, :], scalar=scale[:, m:m + 1], in1=rstd[:, :], op0=ALU.mult, op1=ALU.mult).then_inc(y_ready if final else t_ready, 1)
                    if not final and m >= 1:
                        low_x(m - 1)
                    if m == KT // 2 or n and m == 2:
                        advance(1)
                if not final:
                    low_x(KT - 1)

            def residual(n, factor, tile):
                g = (3 * (n - 1) + 2) * KT
                link(nc.vector.tensor_scalar(coef[:, :], mod[:, g:g + KT], 1.0, factor, ALU.add, ALU.mult))
                for m in range(KT):
                    src = tile(m)
                    nc.vector.scalar_tensor_tensor(out=h[:, m, :], in0=src, scalar=coef[:, m:m + 1], in1=h[:, m, :], op0=ALU.mult, op1=ALU.add).then_inc(h_ready, 1)
                    if 2 <= m <= SQ_V:
                        add_square(n, m - 1)

            def add_ada(sums, n, count, col=0):
                dve.wait_ge(ada_reduced, n + count)
                nc.vector.tensor_tensor(mod[:, 2 * n:2 * (n + count)], sums[:, col:col + 2 * count], adab[:, 2 * n:2 * (n + count)], ALU.add).then_inc(mod_ready, 1)
                mods[0] += 1

            def ffn(f):
                f0, j0 = ffn_chunk0(f), ffn_job0(f)
                n0 = ADA_PLAN.get(f)
                c0 = nxt[0]

                def up(p, parity):
                    dve.wait_ge(gate_free, PAIRS * f + p + 3)
                    dve.wait_ge(chunk_used, f0 + 4 * p + 4)
                    nc.vector.tensor_tensor(gated[:, parity, :], silu_a[:, parity, :], job_bank(j0 + 2 * parity + 1)[:, :], ALU.mult).then_inc(up_free, 1)
                    dve.wait_ge(g_hi_ready, PAIRS * f + p + 1)
                    k = slice(2 * p, 2 * p + 2) if isinstance(p, int) else bass.ds(2 * p, 2)
                    nc.vector.tensor_tensor(g_lo[:, k, :].rearrange("p k t -> p (k t)"), gated[:, parity, :], g_hi[:, k, :].rearrange("p k t -> p (k t)"), ALU.subtract).then_inc(g_lo_ready, 1)

                def ada_step(n, landed, parity, ks, acc, reduced):
                    if ks[0] == 0:
                        dve.wait_ge(ada_landed[parity], landed)
                        dve.wait_ge(ada_reduced, reduced)
                    for k in ks:
                        ada_part(n, ada_raw[:, parity, :, :], acc, k)

                with dve.Fori(0, PAIRS // 2) as t:
                    for parity in range(2):
                        for i in range(4):
                            if has_ada(f):
                                ada_step(n0 + 2 * t + parity, landed_count(n0 + parity) + 16 * t, (n0 + parity) % 2, (2 * i, 2 * i + 1),
                                         ada_acc[:, (n0 + parity) % 2, :], n0 + 2 * t + parity - 1)
                            low(None, (c0 + i) % RING, c0 + 4 * parity + i + 1 + 8 * t)
                        up(2 * t + parity, parity)
                nxt[0] += 8 * (PAIRS // 2)
                if has_ada(f):
                    n = n0 + PAIRS - 1
                    for i in range(4):
                        if i == 2:
                            add_ada(bank[0], n0, PAIRS - 1)
                        ada_step(n, landed_count(n), n % 2, (2 * i, 2 * i + 1), ada_acc[:, n % 2, :], n - 1)
                        advance(1)
                else:
                    advance(4)
                up(PAIRS - 1, 0)
                c0 = nxt[0]
                n1 = n0 + PAIRS if has_ada(f) else None
                steps = min(DOWN_LOOP, (ALL_CHUNKS - c0) // 4)

                def down_step(s, j=0):
                    for i in range(4):
                        if has_ada(f):
                            first = n1 + j
                            ada_step(first + s, landed_count(first) + 8 * s, first % 2, (2 * i, 2 * i + 1),
                                     ada_late[:, bass.ds(s + j, 1), :].rearrange("p n c -> p (n c)"), n0)
                        low(None, (c0 + i) % RING, c0 + 4 * j + i + 1 + 4 * s)
                if f % 2 == 0:
                    dve.wait_ge(ws_landed, 16 * (f // 2 + 1))
                    nc.vector.tensor_tensor(ws_raw[:, :, :], ws_raw[:, :, :], tril[:, :].unsqueeze(1).to_broadcast([P, HEADS, P]), ALU.mult).then_inc(ws_masked, 1)
                if has_ada(f):
                    with dve.Fori(0, DOWN_LOOP // 2) as t:
                        down_step(2 * t)
                        down_step(2 * t, 1)
                    down_step(DOWN_LOOP - 1)
                else:
                    with dve.Fori(0, steps) as t:
                        down_step(t)
                nxt[0] += 4 * steps
                if steps < DOWN_LOOP:
                    advance(2)
                if has_ada(f):
                    add_ada(job_bank(j0 + 2 * (PAIRS - 2)), n1 - 1, 2)
                dve.wait_ge(mod_ready, mods[0])

                def tile(m):
                    if m < KT - 2:
                        dve.wait_ge(down_done, 3 * f + m // 2 + 1)
                    else:
                        dve.wait_ge(chunk_used, f0 + FFN_CHUNKS)
                    return bank[m // 2][:, (m % 2) * T:(m % 2 + 1) * T]
                residual(3 * (f // 2) + 1 + 2 * (f % 2), 0.5, tile)
                norm(3 * (f // 2) + 1 + 2 * (f % 2))
                if has_ada(f):
                    add_ada(bank[3], n1 + 1, LATE - 1)

            def mixer(l):
                c0, j0 = mix_chunk0(l), mix_job0(l)
                m0 = MIX_READS * l
                read = [m0]

                def scored_bank():
                    dve.wait_ge(mix_scored, read[0] + 1)
                    read[0] += 1
                    return bank[(read[0] - m0 - 1) % 4]

                ada_at = [0]

                def ada_next(between=0):
                    ada_block(ADA_MIX[l] + ada_at[0], ada_mix[:, ada_at[0], :], between)
                    ada_at[0] += 1

                fv = [l]

                advance(4)
                ada_next()
                for b in range(2):
                    nc.vector.tensor_copy(ws_t[:, 4 * b:4 * b + 4, :].rearrange("p g t -> p (g t)"), scored_bank()[:, :]).then_inc(mix_read, 1)
                advance(4)
                ada_next()

                f0 = 0 if l == 0 else 4
                dl, fl = flat(decay), flat(logf)
                advance(4)
                dve.wait_ge(f_act, f0 + 4)
                nc.vector.scalar_tensor_tensor(out=fl, in0=fl, scalar=0.0, in1=dl, op0=ALU.min, op1=ALU.subtract).then_inc(f_vec, 1)
                fv[0] += 1
                if l > 0:
                    def per_head(row):
                        return lb_t[:, row, :].unsqueeze(2).to_broadcast([P, HEADS, T])
                    advance(1)
                    dve.wait_ge(f_vec, fv[0])
                    nc.vector.tensor_tensor(logf[:, :, :], logf[:, :, :], per_head(0), ALU.add).then_inc(f_vec, 1)
                    fv[0] += 1
                    advance(1)
                    dve.wait_ge(f_vec, fv[0])
                    nc.vector.tensor_tensor(decay[:, :, :], logf[:, :, :], per_head(1), ALU.subtract).then_inc(f_vec, 1)
                    fv[0] += 1
                    advance(1)
                    nc.vector.tensor_tensor(logf[:, :, :], logf[:, :, :], per_head(1), ALU.max)
                    advance(1)
                    nc.vector.tensor_tensor(key[:, :, :], key[:, :, :], per_head(2), ALU.mult).then_inc(f_vec, 1)
                    fv[0] += 1
                    advance(2)
                    dve.wait_ge(f_act, f0 + 7)
                    dve.wait_ge(f_vec, fv[0])
                    nc.vector.tensor_tensor(logf[:, :, :], logf[:, :, :], decay[:, :, :], ALU.add).then_inc(f_vec, 1)
                    fv[0] += 1
                    advance(1)
                else:
                    advance(2)
                    ada_next(1)
                    advance(1)
                    ada_next()

                def suffix(n, m):
                    pre, d = halves(logf, m), halves(decay, m)
                    mid = pre[:, :, 0, m - 1:m].to_broadcast([P, KT * T // (2 * m), m])
                    if n:
                        dve.wait_ge(vv, chain[0])
                    nc.vector.tensor_tensor(d[:, :, 0, :], mid, pre[:, :, 0, :], ALU.subtract).then_inc(suffix_ready, 1)

                def pairs(n, m):
                    pre, d, w = halves(logf, m), halves(decay, m), halves(pair, m)
                    dve.wait_ge(decay_ready, 16 * l + 2 * n + 2)
                    if n:
                        dve.wait_ge(mix_scored, read[0])
                    nc.vector.tensor_tensor(w[:, :, 0, :], halves(key, m)[:, :, 0, :], d[:, :, 0, :], ALU.mult)
                    nc.vector.tensor_tensor(w[:, :, 1, :], halves(query, m)[:, :, 1, :], d[:, :, 1, :], ALU.mult).then_inc(pair_ready, 1)
                    if m < P:
                        mid = pre[:, :, 0, m - 1:m].to_broadcast([P, KT * T // (2 * m), m])
                        chain[0] += 1
                        nc.vector.tensor_tensor(pre[:, :, 1, :], pre[:, :, 1, :], mid, ALU.add).then_inc(vv, 1)

                def merge(n, m):
                    mask = level_mask[:, n, :].rearrange("p (b m) -> p b m", m=m).unsqueeze(1).to_broadcast([P, 8, HALF // m, m])
                    for b in range(2):
                        src = scored_bank()[:, :].rearrange("p (a b m) -> p a b m", a=8, m=m)
                        s = score[:, 4 * b:4 * b + 4, :].rearrange("p h (n b two m) -> p (h n) b two m", n=NT, two=2, m=m)
                        nc.vector.copy_predicated(s[:, :, :, 1, :], mask, src).then_inc(mix_read, 1)

                dve.wait_ge(f_vec, fv[0])
                suffix(0, 1)
                advance(1 if l else 4)
                for b in range(4):
                    s = score[:, 2 * b:2 * b + 2, :].rearrange("p h (n t) -> p (h n) t", n=NT)
                    src = scored_bank()[:, :].rearrange("p (a t) -> p a t", t=P)
                    nc.vector.tensor_tensor(s, src, ident[:, :].unsqueeze(1).to_broadcast([P, 4, P]), ALU.mult).then_inc(mix_read, 1)
                pairs(0, 1)
                suffix(1, 2)
                advance(4)
                merge(0, 1)
                pairs(1, 2)
                suffix(2, 4)
                advance(2)
                dve.wait_ge(proj_taken, PROJ_JOBS * l + 12)
                vt = v_gate[:, :, :].rearrange("p k t -> p (k t)").rearrange("p (a c) -> p a c", c=P)
                for a in range(16):
                    last = nc.vector.bn_stats(ln_stats[:, a, :], vt[:, a, :])
                link(last)
                for a in range(16):
                    last = nc.vector.bn_aggr(ln_mv[:, a, :], ln_stats[:, a, :])
                last.then_inc(ln_var, 1)
                advance(2)
                merge(1, 2)
                pairs(2, 4)
                suffix(3, 8)
                advance(4)
                merge(2, 4)
                dve.wait_ge(ln_std, l + 1)
                link(nc.vector.reciprocal(ln_rstd[:, :], ln_rstd[:, :]))
                for a in range(16):
                    last = nc.vector.tensor_scalar(vt[:, a, :], vt[:, a, :], ln_mv[:, a, 0:1], ln_rstd[:, a:a + 1], ALU.subtract, ALU.mult)
                last.then_inc(v_norm, 1)
                advance(4)
                if l:
                    ada_next()
                dve.wait_ge(bias_landed, 16 * (l + 1))
                for b in range(4):
                    into = scored_bank()
                    src = into[:, :].rearrange("p (g n t) -> p g n t", g=2, n=NT)
                    bias = mix_bias[:, 2 * b:2 * b + 2, :].unsqueeze(2).to_broadcast([P, 2, NT, P])
                    nc.vector.tensor_tensor(src, src, bias, ALU.add).then_inc(vv, 1)
                    chain[0] += 1
                    if b == 0:
                        dve.wait_ge(proj_taken, PROJ_JOBS * l + 16)
                    dve.wait_ge(vv, chain[0])
                    u = u_gate[:, 2 * b:2 * b + 2, :].rearrange("p k t -> p (k t)")
                    nc.vector.tensor_tensor(u, u, into[:, :], ALU.mult).then_inc(mix_read, 1)
                pairs(3, 8)
                suffix(4, 16)
                advance(4)
                merge(3, 8)
                pairs(4, 16)
                suffix(5, 32)
                advance(2)
                dve.wait_ge(ya_hi_ready, l + 1)
                nc.vector.tensor_tensor(flat(ya_lo), flat(u_gate), flat(ya_hi), ALU.subtract).then_inc(ya_lo_ready, 1)
                advance(2)
                merge(4, 16)
                pairs(5, 32)
                suffix(6, 64)
                advance(4)
                merge(5, 32)
                pairs(6, 64)
                suffix(7, 128)
                advance(4)
                merge(6, 64)
                pairs(7, 128)
                advance(4)
                if l:
                    ada_next()
                for b in range(2):
                    nc.vector.tensor_copy(decay[:, 2 * b:2 * b + 2, :].rearrange("p k t -> p (k t)"), scored_bank()[:, :]).then_inc(mix_read, 1)
                for i in range(4):
                    if i < 3:
                        ada_next()
                    advance(1)
                dve.wait_ge(o_taken, 4 * (l + 1))
                dve.wait_ge(proj_taken, PROJ_JOBS * l + 24)
                nc.vector.tensor_tensor(flat(o_t), flat(o_t), flat(og), ALU.mult).then_inc(vv, 1)
                chain[0] += 1
                advance(2)
                ada_next()
                advance(2)
                dve.wait_ge(o_rms, l + 1)
                dve.wait_ge(vv, chain[0])
                nc.vector.tensor_tensor(flat(o_t), flat(o_t), flat(rms_o), ALU.mult).then_inc(yb_full, 1)
                advance(2)

                def gated_job(jj, gate):
                    q = jj % 4
                    dve.wait_ge(chunk_used, c0 + 64 + 2 * jj + 2)
                    g = gate[:, 2 * q:2 * q + 2, :].rearrange("p k t -> p (k t)")
                    nc.vector.tensor_tensor(g, g, job_bank(j0 + PROJ_JOBS + jj)[:, :], ALU.mult).then_inc(branch_taken, 1)
                    return g

                dve.wait_ge(proj_taken, PROJ_JOBS * (l + 1))
                gated_job(0, ga)
                dve.wait_ge(yb_hi_ready, l + 1)
                nc.vector.tensor_tensor(flat(yb_lo), flat(o_t), flat(yb_hi), ALU.subtract).then_inc(yb_lo_ready, 1)
                advance(2)
                gated_job(1, ga)
                for jj in (2, 3):
                    gated_job(jj, ga)
                    advance(2)
                for q in range(4):
                    g = gated_job(4 + q, gb)
                    dve.wait_ge(branch_taken, 8 * l + 5 + q)
                    a = ga[:, 2 * q:2 * q + 2, :].rearrange("p k t -> p (k t)")
                    nc.vector.tensor_tensor(a, a, g, ALU.add).then_inc(m_full, 1)
                    if q < 3:
                        advance(2)
                    dve.wait_ge(m_hi_ready, 4 * l + q + 1)
                    nc.vector.tensor_tensor(ya_lo[:, 2 * q:2 * q + 2, :].rearrange("p k t -> p (k t)"), a, ya_hi[:, 2 * q:2 * q + 2, :].rearrange("p k t -> p (k t)"), ALU.subtract).then_inc(m_lo_ready, 1)
                advance(2)
                add_ada(bank[1], ADA_MIX[l], MIX_BLOCKS)
                dve.wait_ge(mod_ready, mods[0])

                def tile(m):
                    jj = 8 + m // 2
                    if m % 2 == 0:
                        if m:
                            advance(2)
                        dve.wait_ge(chunk_used, c0 + 64 + 2 * jj + 2)
                    return job_bank(j0 + PROJ_JOBS + jj)[:, (m % 2) * T:(m % 2 + 1) * T]
                residual(3 * l + 2, 1.0, tile)
                norm(3 * l + 2)

            norm(0)
            dve.wait_ge(const_landed, 32)
            nc.vector.tensor_copy(level_mask[:, :, :], mask_in[:, :, :])
            for l in range(DEPTH):
                ffn(2 * l)
                mixer(l)
                ffn(2 * l + 1)

        @block.tensor
        def _(pe):
            def mm(out_, lhs, rhs, start, stop=False):
                return nc.tensor.matmul(out_, lhs, rhs, start=start, stop=stop, skip_group_check=True)

            def tiles(slot, k, m):
                at = k * JC + m * P
                return w_hi[:, slot, at:at + P], w_lo[:, slot, at:at + P]

            def three(out_, w, xs, start):
                (wh, wl), (xh, xl) = w, xs
                mm(out_, wh, xh, start)
                mm(out_, wh, xl, False)
                return mm(out_, wl, xh, False)

            def first_jobs(banks, at, n):
                for kk in range(KT):
                    q, k = kk // KC, kk % KC
                    if k == 0:
                        pe.wait_ge(lo_ready, at + 2 * q + 2)
                    pe.wait_ge(x_hi_ready, KT * n + kk + 1)
                    for j, b in enumerate(banks):
                        for m in range(2):
                            wh, wl = tiles((at + 2 * q + j) % RING, k, m)
                            dst = b[:, m * T:(m + 1) * T]
                            mm(dst, wh, x_hi[:, kk, :], kk == 0 and m == 0)
                            last = mm(dst, wl, x_hi[:, kk, :], False)
                    pe.wait_ge(x_lo_ready, KT * n + kk + 1)
                    for j, b in enumerate(banks):
                        for m in range(2):
                            wh, _ = tiles((at + 2 * q + j) % RING, k, m)
                            last = mm(b[:, m * T:(m + 1) * T], wh, x_lo[:, kk, :], False)
                    if k == KC - 1:
                        last.then_inc(chunk_used, 2)

            def job(b, slot0, waits, src, token_major=False, ready=None):
                hi, lo = src
                for q in range(2):
                    slot = (slot0 + q) % RING
                    pe.wait_ge(lo_ready, waits[q])
                    for k in range(KC):
                        kk = KC * q + k
                        if ready is not None:
                            pe.wait_ge(ready[0], ready[1] + kk // ready[2] + 1)
                        for m in range(2):
                            start = kk == 0 and m == 0
                            dst = b[:, m * T:(m + 1) * T]
                            if token_major:
                                at = k * JC
                                whl = w_hi[:, slot, at:at + JC], w_lo[:, slot, at:at + JC]
                                xt = hi[:, kk, m * P:(m + 1) * P], lo[:, kk, m * P:(m + 1) * P]
                                mm(dst, xt[0], whl[0], start)
                                mm(dst, xt[0], whl[1], False)
                                last = mm(dst, xt[1], whl[0], False)
                            else:
                                last = three(dst, tiles(slot, k, m), (hi[:, kk, :], lo[:, kk, :]), start)
                    if q == 0:
                        last.then_inc(chunk_used, 1)
                return last

            def reduce_block(n, acc, b, col):
                pe.wait_ge(ada_summed, KT * n + KT)
                for m in range(2):
                    dst = b[:, col + m:col + m + 1] if isinstance(col, int) else b[:, bass.ds(col + m, 1)]
                    last = mm(dst, acc[:, m * P:(m + 1) * P], ones[:, 0:1], True, True)
                last.then_inc(ada_reduced, 1)

            def norm_sum(n):
                pe.wait_ge(sq_summed, n + 1)
                mm(norm_bank[n][:, 0:T], ones[:, :], norm_tmp[:, 0, :], True)
                for m in range(SQ_V, KT):
                    pe.wait_ge(sq_ready, KT * n + m + 1)
                    last = mm(norm_bank[n][:, 0:T], ones[:, :], norm_tmp[:, m, :], False, m == KT - 1)
                last.then_inc(sum_ready, 1)

            pe.wait_ge(small_landed, 96)
            pe.wait_ge(ones_ready, 1)
            nc.tensor.transpose(bank[1][:, 0:ROWS], rows_in[0:ROWS, 0, :], ident[0:ROWS, 0:ROWS])
            for l in range(DEPTH):
                last = nc.tensor.transpose(bank[1][:, P + 72 * l:P + 72 * (l + 1)], rows_in[0:72, 1 + l, :], ident[0:72, 0:72])
            last.then_inc(rows_turned, 1)

            def turn_x():
                pe.wait_ge(x_landed, 16)
                for q in range(4):
                    for i in range(4):
                        k, n = 2 * q + i // 2, i % 2
                        last = nc.tensor.transpose(bank[4 + q][:, i * P:(i + 1) * P], x_in[:, n, k * P:(k + 1) * P], ident[:, :])
                    last.then_inc(x_turned, 1)

            def turn_row(i):
                pe.wait_ge(row_copied, i + 1)
                n = EARLY_V + i
                for m in range(2):
                    last = mm(bank[0][:, 2 * n + m:2 * n + m + 1], early_row[0:1, i, m * P:(m + 1) * P], ones[0:1, 0:1], True, True)
                last.then_inc(ada_reduced, 1)

            pe.wait_ge(c_ready, 1)
            for n in range(EARLY_V):
                pe.wait_ge(early_landed[EARLY_V + n], 16)
                for k in range(KT):
                    last = mm(row_bank(n)[0:1, 0:256], c_act[:, k:k + 1], early(EARLY_V + n)[:, k, :], k == 0, k == KT - 1)
                last.then_inc(row_summed, 1)
                if n == 0:
                    turn_x()
                else:
                    turn_row(n - 1)
                if n == 1:
                    norm_sum(0)
                reduce_block(n, early_acc[:, n, :], bank[0], 2 * n)
            turn_row(EARLY_V - 1)
            for _ in range(WARM_START):
                mm(bank[3][:, :], ident[:, :], x_in[:, 0, 0:512], True, True)

            def stay_warm(count, tile, b):
                for _ in range(count):
                    mm(b[:, :], tile[:, 0, 0:P], tile[:, 0:2, :].rearrange("p k t -> p (k t)"), True, True)

            def ffn(f):
                c0, j0 = ffn_chunk0(f), ffn_job0(f)
                n0 = ADA_PLAN.get(f)
                n = 3 * (f // 2) + 2 * (f % 2)
                src = (x_hi, x_lo)

                def do_pair(p, parity):
                    for i, free in enumerate((gate_free, up_free)):
                        pe.wait_ge(free, PAIRS * f + p + 1)
                        at = c0 + 4 * p + 2 * i + 1
                        last = job(job_bank(j0 + 2 * parity + i), c0 + 2 * i, (at, at + 1), src)
                        last.then_inc(chunk_used, 1)
                        if has_ada(f) and i == 0:
                            reduce_block(n0 + p - 1, ada_acc[:, (n0 + parity + 1) % 2, :], bank[0], 2 * p - 2)

                pe.wait_ge(gate_free, PAIRS * f + 1)
                pe.wait_ge(up_free, PAIRS * f + 1)
                first_jobs((job_bank(j0), job_bank(j0 + 1)), c0, n)
                with pe.Fori(0, PAIRS // 2) as t:
                    do_pair(2 * t + 1, 1)
                    do_pair(2 * t + 2, 0)

                if has_ada(f):
                    pe.wait_ge(mod_ready, mod_count(f))
                d0 = c0 + 4 * PAIRS

                def down_tile(k, slot, m, start):
                    ks = slice(k, k + 1) if isinstance(k, int) else bass.ds(k, 1)
                    hi = g_hi[:, ks, :].rearrange("p k t -> p (k t)")
                    lo = g_lo[:, ks, :].rearrange("p k t -> p (k t)")
                    w = w_hi[:, slot, m * P:(m + 1) * P], w_lo[:, slot, m * P:(m + 1) * P]
                    return three(bank[m // 2][:, (m % 2) * T:(m % 2 + 1) * T], w, (hi, lo), start)

                n1 = n0 + PAIRS if has_ada(f) else None
                sums = job_bank(j0 + 2 * (PAIRS - 2))
                if has_ada(f):
                    pe.wait_ge(gate_free, PAIRS * f + PAIRS + 1)

                def down_step(t, first=False):
                    for i in range(4):
                        pe.wait_ge(lo_ready, d0 + 4 * t + i + 1)
                        pe.wait_ge(g_lo_ready, PAIRS * f + 2 * t + i // 2 + 1)
                        for m in range(KT):
                            last = down_tile(4 * t + i, (d0 + i) % RING, m, first and i == 0 and m % 2 == 0)
                        last.then_inc(chunk_used, 1)
                        if has_ada(f) and first and i == 1:
                            reduce_block(n1 - 1, ada_acc[:, (n1 - 1) % 2, :], sums, 0)
                down_step(0, True)
                with pe.Fori(1, DOWN_LOOP) as t:
                    down_step(t)
                pe.wait_ge(lo_ready, d0 + HT)
                pe.wait_ge(g_lo_ready, PAIRS * (f + 1))
                for m in range(KT):
                    for k in (HT - 2, HT - 1):
                        last = down_tile(k, (d0 + k) % RING, m, False)
                    if m == KT - 1:
                        last.then_inc(chunk_used, 2)
                    elif m % 2:
                        last.then_inc(down_done, 1)
                    if m == 0 and has_ada(f):
                        reduce_block(n1, ada_late[:, 0, :], sums, 2)
                norm_sum(n + 1)
                for i in range(1, LATE if has_ada(f) else 0):
                    reduce_block(n1 + i, ada_late[:, i, :], bank[3], 2 * i - 2)
                if f % 2:
                    stay_warm(WARM[1] if f < 2 * DEPTH - 1 else WARM[3], g_hi, bank[1])

            def mod_count(f):
                return {0: 2, 1: 6, 2: 9}[f]

            def mixer(l):
                c0, j0 = mix_chunk0(l), mix_job0(l)
                m0 = MIX_READS * l
                done = [m0]
                src = (x_hi, x_lo)

                def group(g, token_major=False):
                    for j in (2 * g, 2 * g + 1):
                        if j >= 4:
                            pe.wait_ge(proj_taken, PROJ_JOBS * l + j - 3)
                        at = c0 + 2 * j
                        last = job(job_bank(j0 + j), at, (at + 1, at + 2), src, token_major)
                        last.then_inc(chunk_used, 1)

                def next_bank():
                    if done[0] >= m0 + 4:
                        pe.wait_ge(mix_read, done[0] - 3)
                    done[0] += 1
                    return bank[(done[0] - m0 - 1) % 4]

                def score_diagonal():
                    for b in range(4):
                        dst = next_bank()
                        for i in range(4):
                            hh, nn = 2 * b + i // 2, i % 2
                            at = slice(nn * P, (nn + 1) * P)
                            last = mm(dst[:, i * P:(i + 1) * P], key[:, hh, at], query[:, hh, at], True, True)
                        last.then_inc(mix_scored, 1)

                def score_level(m):
                    for b in range(2):
                        dst = next_bank()
                        for i in range(8):
                            hh, nn = 4 * b + i // 2, i % 2
                            at = slice(nn * P, (nn + 1) * P)
                            upper = pair[:, hh, at].rearrange("p (b two m) -> p b two m", two=2, m=m)[:, :, 1, :]
                            last = mm(dst[:, i * HALF:(i + 1) * HALF].rearrange("p (b m) -> p b m", m=m), pair[:, hh, at], upper, True, True)
                        last.then_inc(mix_scored, 1)

                pe.wait_ge(ws_masked, l + 1)
                for b in range(2):
                    dst = next_bank()
                    for i in range(4):
                        last = nc.tensor.transpose(dst[:, i * P:(i + 1) * P], ws_raw[:, 4 * b + i, :], ident[:, :])
                    last.then_inc(mix_scored, 1)
                stay_warm(WARM[0], g_hi, bank[2])
                first_jobs((job_bank(j0), job_bank(j0 + 1)), c0, 3 * l + 1)
                for g in (1, 2, 3):
                    group(g)
                group(4, True)
                pe.wait_ge(proj_taken, PROJ_JOBS * l + 8)
                pe.wait_ge(f_vec, 1 if l == 0 else 5)
                score_diagonal()
                for n in range(3):
                    group(5 + n, n == 0)
                    pe.wait_ge(pair_ready, 8 * l + n + 1)
                    score_level(2 ** n)
                group(8, True)
                pe.wait_ge(v_norm, l + 1)
                vt = v_gate[:, :, :].rearrange("p k t -> p (k t)").rearrange("p (n g c) -> p n g c", n=NT, c=P)
                for b in range(4):
                    into = next_bank()
                    for i in range(4):
                        g, nn = 2 * b + i // 2, i % 2
                        last = mm(into[:, i * P:(i + 1) * P], vt[:, nn, g, :], ws_t[:, g, :], True, True)
                    last.then_inc(mix_scored, 1)
                for n in range(3, 7):
                    group(6 + n, n == 3)
                    pe.wait_ge(pair_ready, 8 * l + n + 1)
                    score_level(2 ** n)
                group(13)
                pe.wait_ge(pair_ready, 8 * l + 8)
                for b in range(2):
                    dst = next_bank()
                    for i in range(4):
                        hh = 4 * b + i
                        last = mm(dst[:, i * P:(i + 1) * P], pair[:, hh, 0:P], pair[:, hh, P:2 * P], True, True)
                    last.then_inc(mix_scored, 1)
                group(14)
                pe.wait_ge(mix_read, m0 + MIX_READS)
                vv_ = val[:, :, :].rearrange("p k t -> p (k t)").rearrange("p (n h c) -> p n h c", n=NT, c=P)
                cross = decay[:, 0:4, :].rearrange("p k (a t) -> p (k a) t", t=P)
                for b in range(4):
                    for i in range(4):
                        hh, nn = 2 * b + i // 2, i % 2
                        dst = bank[b][:, i * P:(i + 1) * P]
                        last = mm(dst, vv_[:, nn, hh, :], score[:, hh, nn * P:(nn + 1) * P], True, nn == 0)
                        if nn == 1:
                            last = mm(dst, vv_[:, 0, hh, :], cross[:, hh, :], False, True)
                    last.then_inc(o_done, 1)
                group(15)
                for b in range(4):
                    pe.wait_ge(o_taken, 4 * l + b + 1)
                    mm(bank[b][:, :], ones[:, :], sq_o[:, 2 * b:2 * b + 2, :].rearrange("p k t -> p (k t)"), True, True).then_inc(o_summed, 1)

                def out_jobs(b, operand, ready, count, tiles_per_count=None):
                    for q in range(4):
                        jj = 4 * b + q
                        if jj < 4:
                            pe.wait_ge(proj_taken, PROJ_JOBS * l + PROJ_JOBS - 3 + jj)
                        else:
                            pe.wait_ge(branch_taken, 8 * l + jj - 3)
                        if q == 0 and not tiles_per_count:
                            pe.wait_ge(ready, count)
                        at = c0 + 64 + 2 * jj
                        job(job_bank(j0 + PROJ_JOBS + jj), at, (at + 1, at + 2), operand,
                            ready=(ready, count, tiles_per_count) if q == 0 and tiles_per_count else None).then_inc(chunk_used, 1)
                        if b == 1:
                            pe.wait_ge(o_rms, l + 1)
                            for i in (2 * q, 2 * q + 1):
                                reduce_block(ADA_MIX[l] + i, ada_mix[:, i, :], bank[1], 2 * i)
                out_jobs(0, (ya_hi, ya_lo), ya_lo_ready, l + 1)
                out_jobs(1, (yb_hi, yb_lo), yb_lo_ready, l + 1)
                out_jobs(2, (ya_hi, ya_lo), m_lo_ready, 4 * l, 2)
                norm_sum(3 * l + 2)
                stay_warm(WARM[2], ya_hi, bank[1])

            for l in range(DEPTH):
                ffn(2 * l)
                mixer(l)
                ffn(2 * l + 1)
            for n in range(NT):
                for q in range(4):
                    for i in range(2):
                        k = 2 * q + i
                        pe.wait_ge(y_ready, k + 1)
                        last = nc.tensor.transpose(bank[4 * n + q][:, i * P:(i + 1) * P], y_t[:, k, n * P:(n + 1) * P], ident[:, :])
                    last.then_inc(y_turned, 1)


_INS = ['x', 'c', 'w_in', 'gmlp_ws', 'gmlp_b', 'hgrn_lb_logits', 'w_branch_a', 'w_branch_b', 'w_out',
        'ffn_w13', 'ffn_w2', 'norm_w', 'ada_w', 'ada_b', 'final_norm_w']


def _constants():
    i = np.arange(P)
    s, t = i[:, None], i[None, :]
    masks = [((s // (2 * m) == t // (2 * m)) & (s % (2 * m) < m))[:, i % (2 * m) >= m] for m in LEVELS]
    return {
        'ident': np.eye(P, dtype=np.float32),
        'level_mask': np.ascontiguousarray(np.stack(masks, 1).astype(np.float32)),
        'tril': np.tril(np.ones((P, P), np.float32)),
    }


def kernel(**inputs):
    import concourse.bacc as _bacc
    from concourse.bass_utils import run_bass_kernel_spmd as _run

    nc = _bacc.Bacc("TRN2", target_bir_lowering=False, num_devices=1)
    arrays = {f"in_{n}": np.ascontiguousarray(inputs[n]) for n in _INS}
    arrays.update({f"const_{n}": a for n, a in _constants().items()})
    args = [nc.dram_tensor(n, a.shape, mybir.dt.from_np(a.dtype), kind="ExternalInput").ap() for n, a in arrays.items()]
    args.append(nc.dram_tensor("y", (1, T, D), F32, kind="ExternalOutput").ap())
    trunk(nc, *args)
    r = _run(nc, [arrays], core_ids=[0])
    return r.results[0]["y"]
```
